# Optimizing a Trainium2 kernel written in Bass

```python
import math
import jax, jax.numpy as jnp
from jax import lax
import numpy as np

D_MODEL = 1024
BATCH = 1
SEQ = 256
DEPTH = 2

PL_DIM = 256
N_EVEN = (DEPTH + 1) // 2
N_ODD = DEPTH // 2
CONV_A_WIDTH = D_MODEL
CONV_A_KERNEL = 3
GDN_HEADS = 8
GDN_HEAD_DIM = 128
GDN_WIDTH = GDN_HEADS * GDN_HEAD_DIM
GDN_CONV_KERNEL = 4
GDN_CHUNK = 64
HGRN_HEAD_DIM = 128
HGRN_WIDTH = 2 * D_MODEL
HGRN_HEADS = HGRN_WIDTH // HGRN_HEAD_DIM
HGRN_CHUNK = 32
EVEN_IN = 4 * CONV_A_WIDTH + 4 * GDN_WIDTH + 2 * GDN_HEADS
EVEN_MIX = CONV_A_WIDTH + GDN_WIDTH
ODD_IN = 4 * HGRN_WIDTH
ODD_MIX = HGRN_WIDTH
DEEPNORM_ALPHA = (2.0 * DEPTH) ** 0.25
DEEPNORM_BETA = (8.0 * DEPTH) ** -0.25
NORM_EPS = 1e-5


def layer_norm(x, g, b):
    xf = x.astype(jnp.float32)
    mu = jnp.mean(xf, axis=-1, keepdims=True)
    var = jnp.mean(jnp.square(xf - mu), axis=-1, keepdims=True)
    return ((xf - mu) * lax.rsqrt(var + NORM_EPS) * g.astype(jnp.float32) + b.astype(jnp.float32)).astype(x.dtype)

def rms_norm(x, g):
    xf = x.astype(jnp.float32)
    y = xf * lax.rsqrt(jnp.mean(jnp.square(xf), axis=-1, keepdims=True) + NORM_EPS)
    return (y * g.astype(jnp.float32)).astype(x.dtype)

def l2_normalize(x):
    xf = x.astype(jnp.float32)
    return (xf * lax.rsqrt(jnp.sum(jnp.square(xf), axis=-1, keepdims=True) + 1e-6)).astype(x.dtype)

def causal_depthwise_conv(x, w):
    k, c = w.shape
    return lax.conv_general_dilated(
        x, w[:, None, :].astype(x.dtype), window_strides=(1,), padding=[(k - 1, 0)],
        dimension_numbers=("NWC", "WIO", "NWC"), feature_group_count=c)

def _to_chunks(t, c):
    b, s, h, d = t.shape
    return t.reshape(b, s // c, c, h, d).transpose(0, 3, 1, 2, 4)

def _from_chunks(t):
    b, h, n, c, d = t.shape
    return t.transpose(0, 2, 3, 1, 4).reshape(b, n * c, h, d)

def gated_delta_rule(q, k, v, g, beta):
    dtype = v.dtype
    c = GDN_CHUNK
    dk, dv = q.shape[-1], v.shape[-1]
    q = _to_chunks(q.astype(jnp.float32) * (dk ** -0.5), c)
    k = _to_chunks(k.astype(jnp.float32), c)
    v = _to_chunks(v.astype(jnp.float32), c)
    g = _to_chunks(g.astype(jnp.float32)[..., None], c)[..., 0]
    beta = _to_chunks(beta.astype(jnp.float32)[..., None], c)
    gc = jnp.cumsum(g, axis=-1)
    incl = jnp.tril(jnp.ones((c, c), bool))
    strict = jnp.tril(jnp.ones((c, c), bool), -1)
    decay = jnp.exp(jnp.where(incl, gc[..., :, None] - gc[..., None, :], -jnp.inf))
    kb = k * beta
    low = jnp.where(strict, jnp.einsum("bhnid,bhnjd->bhnij", kb, k) * decay, 0.0)
    rhs = jnp.concatenate([v * beta, kb * jnp.exp(gc)[..., None]], axis=-1)
    sol = lax.linalg.triangular_solve(low + jnp.eye(c, dtype=jnp.float32), rhs,
                                      left_side=True, lower=True, unit_diagonal=True)
    u, w = sol[..., :dv], sol[..., dv:]
    attn = jnp.einsum("bhnid,bhnjd->bhnij", q, k) * decay
    q_dec = q * jnp.exp(gc)[..., None]
    g_last = gc[..., -1]
    k_dec = k * jnp.exp(g_last[..., None] - gc)[..., None]

    def step(state, xs):
        q_i, k_i, u_i, w_i, a_i, gl_i = xs
        v_new = u_i - jnp.einsum("bhcd,bhde->bhce", w_i, state)
        o_i = jnp.einsum("bhcd,bhde->bhce", q_i, state) + jnp.einsum("bhij,bhje->bhie", a_i, v_new)
        state = state * jnp.exp(gl_i)[..., None, None] + jnp.einsum("bhcd,bhce->bhde", k_i, v_new)
        return state, o_i

    mv = lambda t: jnp.moveaxis(t, 2, 0)
    s0 = jnp.zeros(q.shape[:2] + (dk, dv), jnp.float32)
    _, o = lax.scan(step, s0, (mv(q_dec), mv(k_dec), mv(u), mv(w), mv(attn), mv(g_last)))
    return _from_chunks(jnp.moveaxis(o, 0, 2)).astype(dtype)

def hgrn2_recurrence(q, k, v, logf):
    dtype = v.dtype
    c = HGRN_CHUNK
    q, k, v, logf = (jnp.moveaxis(_to_chunks(t.astype(jnp.float32), c), 2, 0) for t in (q, k, v, logf))
    b = jnp.cumsum(logf, axis=-2)
    incl = jnp.tril(jnp.ones((c, c), bool))[:, :, None]

    def step(state, xs):
        q_i, k_i, v_i, b_i = xs
        b_last = b_i[..., -1:, :]
        decay = jnp.exp(jnp.where(incl, b_i[..., :, None, :] - b_i[..., None, :, :], -jnp.inf))
        attn = jnp.einsum("bhtd,bhsd,bhtsd->bhts", q_i, k_i, decay)
        o_i = (jnp.einsum("bhtd,bhde->bhte", q_i * jnp.exp(b_i), state)
               + jnp.einsum("bhts,bhse->bhte", attn, v_i))
        state = (state * jnp.exp(b_last)[..., 0, :, None]
                 + jnp.einsum("bhsd,bhse->bhde", k_i * jnp.exp(b_last - b_i), v_i))
        return state, o_i

    s0 = jnp.zeros(q.shape[1:3] + (q.shape[-1], v.shape[-1]), jnp.float32)
    _, o = lax.scan(step, s0, (q, k, v, b))
    return _from_chunks(jnp.moveaxis(o, 0, 2)).astype(dtype)

def conv_gdn_mixer(x, w_in, conv_a_w, conv_b_w, a_log, dt_bias, gdn_norm_g, w_out):
    bsz, s, _ = x.shape
    wa, wg, h = CONV_A_WIDTH, GDN_WIDTH, GDN_HEADS
    proj = x @ w_in
    cuts = [wa, 2 * wa, 3 * wa, 4 * wa, 4 * wa + 3 * wg, 4 * wa + 4 * wg, 4 * wa + 4 * wg + h]
    h_a, c_a, b_a, z_a, qkv, z_b, beta_raw, a_raw = jnp.split(proj, cuts, axis=-1)
    y_a = b_a * causal_depthwise_conv(c_a * h_a, conv_a_w) * jax.nn.silu(z_a)
    qkv = jax.nn.silu(causal_depthwise_conv(qkv, conv_b_w))
    q, k, v = (t.reshape(bsz, s, h, GDN_HEAD_DIM) for t in jnp.split(qkv, 3, axis=-1))
    q, k = l2_normalize(q), l2_normalize(k)
    beta = jax.nn.sigmoid(beta_raw.astype(jnp.float32))
    g = -jnp.exp(a_log.astype(jnp.float32)) * jax.nn.softplus(a_raw.astype(jnp.float32) + dt_bias.astype(jnp.float32))
    o = gated_delta_rule(q, k, v, g, beta)
    o = rms_norm(o, gdn_norm_g) * jax.nn.silu(z_b.reshape(bsz, s, h, GDN_HEAD_DIM))
    y = jnp.concatenate([y_a, o.reshape(bsz, s, wg)], axis=-1)
    return y @ w_out

def hgrn2_mixer(x, w_in, lower_bound, hgrn_norm_g, w_out):
    bsz, s, _ = x.shape
    q_raw, f_raw, i_in, z = jnp.split(x @ w_in, 4, axis=-1)
    f = lower_bound + (1.0 - lower_bound) * jax.nn.sigmoid(f_raw.astype(jnp.float32))
    q = jax.nn.silu(q_raw)
    k = (1.0 - f).astype(x.dtype)
    logf = jnp.log(f)
    heads = lambda t: t.reshape(bsz, s, HGRN_HEADS, HGRN_HEAD_DIM)
    o = hgrn2_recurrence(heads(q), heads(k), heads(i_in), heads(logf))
    o = rms_norm(o, hgrn_norm_g) * jax.nn.silu(heads(z))
    return o.reshape(bsz, s, HGRN_WIDTH) @ w_out

def first_inputs(seed: int = 0) -> dict:
    key = jax.random.key(seed)
    ks = jax.random.split(key, 20)
    nrm = lambda k, shape, scale: jax.random.normal(k, shape, jnp.float32) * scale
    dt = jnp.exp(jax.random.uniform(ks[6], (N_EVEN, GDN_HEADS), jnp.float32)
                 * (math.log(0.1) - math.log(0.001)) + math.log(0.001))
    return {
        "x": nrm(ks[0], (BATCH, SEQ, D_MODEL), 1.0),
        "p": nrm(ks[1], (DEPTH, BATCH, SEQ, PL_DIM), 1.0),
        "w_in_even": nrm(ks[2], (N_EVEN, D_MODEL, EVEN_IN), D_MODEL ** -0.5),
        "conv_a_w": nrm(ks[3], (N_EVEN, CONV_A_KERNEL, CONV_A_WIDTH), CONV_A_KERNEL ** -0.5),
        "conv_b_w": nrm(ks[4], (N_EVEN, GDN_CONV_KERNEL, 3 * GDN_WIDTH), GDN_CONV_KERNEL ** -0.5),
        "a_log": jnp.log(jax.random.uniform(ks[5], (N_EVEN, GDN_HEADS), jnp.float32, 1.0, 16.0)),
        "dt_bias": dt + jnp.log(-jnp.expm1(-dt)),
        "gdn_norm_g": 1.0 + nrm(ks[7], (N_EVEN, GDN_HEAD_DIM), 0.02),
        "w_out_even": nrm(ks[8], (N_EVEN, EVEN_MIX, D_MODEL), EVEN_MIX ** -0.5 * DEEPNORM_BETA),
        "w_in_odd": nrm(ks[9], (N_ODD, D_MODEL, ODD_IN), D_MODEL ** -0.5),
        "lower_bounds": nrm(ks[10], (DEPTH, HGRN_WIDTH), 0.1),
        "hgrn_norm_g": 1.0 + nrm(ks[11], (N_ODD, HGRN_HEAD_DIM), 0.02),
        "w_out_odd": nrm(ks[12], (N_ODD, ODD_MIX, D_MODEL), ODD_MIX ** -0.5 * DEEPNORM_BETA),
        "ln_g": 1.0 + nrm(ks[13], (DEPTH, D_MODEL), 0.02),
        "ln_b": nrm(ks[14], (DEPTH, D_MODEL), 0.02),
        "w_pl": nrm(ks[15], (DEPTH, PL_DIM, D_MODEL), PL_DIM ** -0.5),
        "w_pl_gate": nrm(ks[16], (DEPTH, D_MODEL, D_MODEL), D_MODEL ** -0.5),
    }

def first_block(x, p, w_in_even, conv_a_w, conv_b_w, a_log, dt_bias, gdn_norm_g, w_out_even,
              w_in_odd, lower_bounds, hgrn_norm_g, w_out_odd, ln_g, ln_b, w_pl, w_pl_gate):
    lbs = jnp.cumsum(jax.nn.softmax(lower_bounds.astype(jnp.float32), axis=0), axis=0)
    lbs = lbs - lbs[0]
    for i in range(DEPTH):
        j = i // 2
        if i % 2 == 0:
            s = conv_gdn_mixer(x, w_in_even[j], conv_a_w[j], conv_b_w[j], a_log[j], dt_bias[j],
                               gdn_norm_g[j], w_out_even[j])
        else:
            s = hgrn2_mixer(x, w_in_odd[j], lbs[i], hgrn_norm_g[j], w_out_odd[j])
        x = layer_norm(DEEPNORM_ALPHA * x + s, ln_g[i], ln_b[i])
        gate = jax.nn.sigmoid((x @ w_pl_gate[i]).astype(jnp.float32))
        x = x + ((p[i] @ w_pl[i]).astype(jnp.float32) * gate).astype(x.dtype)
    return x


DEPTH_2 = 1

N_MIXERS = 3
RMS_EPS = 1e-6
BLOCK = 128
NEG = -1e30

SWA_HEAD_DIM = 64
SWA_HEADS = D_MODEL // SWA_HEAD_DIM
SWA_KV_HEADS = SWA_HEADS // 8
SWA_GROUP = SWA_HEADS // SWA_KV_HEADS
WINDOW = 128

SB_HEAD_DIM = 64
SB_HEADS = D_MODEL // SB_HEAD_DIM

RET_QK_DIM = 256
RET_HEADS = D_MODEL // RET_QK_DIM
RET_V_DIM = 2 * RET_QK_DIM

D_FF = 4 * D_MODEL

N_A = len(range(0, DEPTH_2, N_MIXERS))
N_B = len(range(1, DEPTH_2, N_MIXERS))
N_C = len(range(2, DEPTH_2, N_MIXERS))


def rms_norm_2(x, g):
    xf = x.astype(jnp.float32)
    y = xf * lax.rsqrt(jnp.mean(xf * xf, axis=-1, keepdims=True) + RMS_EPS)
    return (y * g.astype(jnp.float32)).astype(x.dtype)

def alibi_slopes(n_heads):
    return jnp.exp2(-8.0 * jnp.arange(1, n_heads + 1, dtype=jnp.float32) / n_heads)

def swa_mixer(h, w_qkv, sinks, w_o):
    B_, T, _ = h.shape
    nb = T // BLOCK
    HD, KV, G = SWA_HEAD_DIM, SWA_KV_HEADS, SWA_GROUP
    qkv = h @ w_qkv
    q, k, v = jnp.split(qkv, [SWA_HEADS * HD, (SWA_HEADS + KV) * HD], axis=-1)
    q = q.reshape(B_, nb, BLOCK, KV, G, HD)
    k = k.reshape(B_, nb, BLOCK, KV, HD)
    v = v.reshape(B_, nb, BLOCK, KV, HD)

    def with_prev(a):
        prev = jnp.pad(a, ((0, 0), (1, 0), (0, 0), (0, 0), (0, 0)))[:, :-1]
        return jnp.concatenate([prev, a], axis=2)

    kb, vb = with_prev(k), with_prev(v)
    s = jnp.einsum('bnqkgd,bnskd->bnkgqs', q, kb).astype(jnp.float32) * (HD ** -0.5)

    blk = jnp.arange(nb)[:, None, None]
    qi = jnp.arange(BLOCK)[None, :, None]
    kj = jnp.arange(2 * BLOCK)[None, None, :]
    dist = BLOCK + qi - kj
    kpos = (blk - 1) * BLOCK + kj
    mask = (dist >= 0) & (dist < WINDOW) & (kpos >= 0)
    slopes = alibi_slopes(SWA_HEADS).reshape(1, 1, KV, G, 1, 1)
    bias = -slopes * dist.astype(jnp.float32)[None, :, None, None]
    logits = jnp.where(mask[None, :, None, None], s + bias, NEG)

    sink = sinks.astype(jnp.float32).reshape(1, 1, KV, G, 1, 1)
    m = jnp.maximum(jnp.max(logits, axis=-1, keepdims=True), sink)
    p = jnp.exp(logits - m)
    probs = p / (jnp.sum(p, axis=-1, keepdims=True) + jnp.exp(sink - m))
    o = jnp.einsum('bnkgqs,bnskd->bnqkgd', probs.astype(vb.dtype), vb)
    return o.reshape(B_, T, SWA_HEADS * HD) @ w_o

def stick_breaking_mixer(h, w_qkv, w_o):
    B_, T, _ = h.shape
    HD, H = SB_HEAD_DIM, SB_HEADS
    qkv = (h @ w_qkv).reshape(B_, T, 3, H, HD)
    q = jnp.transpose(qkv[:, :, 0], (0, 2, 1, 3))
    k = jnp.transpose(qkv[:, :, 1], (0, 2, 1, 3))
    v = jnp.transpose(qkv[:, :, 2], (0, 2, 1, 3))
    scale = HD ** -0.5
    outs = []
    for n in range(T // BLOCK):
        q0, end = n * BLOCK, (n + 1) * BLOCK
        z = jnp.einsum('bhqd,bhsd->bhqs', q[:, :, q0:end], k[:, :, :end]).astype(jnp.float32) * scale
        t_pos = q0 + jnp.arange(BLOCK)[:, None]
        s_pos = jnp.arange(end)[None, :]
        causal = (s_pos < t_pos)[None, None]
        log_beta = jax.nn.log_sigmoid(z)
        log_1m_beta = jnp.where(causal, jax.nn.log_sigmoid(-z), 0.0)
        rest = lax.cumsum(log_1m_beta, axis=3, reverse=True) - log_1m_beta
        a = jnp.where(causal, jnp.exp(log_beta + rest), 0.0)
        outs.append(jnp.einsum('bhqs,bhsd->bhqd', a.astype(v.dtype), v[:, :, :end]))
    o = jnp.concatenate(outs, axis=2)
    return jnp.transpose(o, (0, 2, 1, 3)).reshape(B_, T, H * HD) @ w_o

def retention_mixer(h, w_in, w_o):
    B_, T, _ = h.shape
    nc, C, H, dk, dv = T // BLOCK, BLOCK, RET_HEADS, RET_QK_DIM, RET_V_DIM
    proj = h @ w_in
    q, k, v, g = jnp.split(proj, [H * dk, 2 * H * dk, 2 * H * dk + H * dv], axis=-1)
    q = q.astype(jnp.float32).reshape(B_, nc, C, H, dk)
    k = k.astype(jnp.float32).reshape(B_, nc, C, H, dk) * (dk ** -0.5)
    v = v.astype(jnp.float32).reshape(B_, nc, C, H, dv)

    log_gamma = jnp.log1p(-jnp.exp2(-5.0 - jnp.arange(H, dtype=jnp.float32)))
    idx = jnp.arange(C)
    diff = idx[:, None] - idx[None, :]
    decay_mat = jnp.where(diff >= 0,
                          jnp.exp(log_gamma[:, None, None] * jnp.maximum(diff, 0).astype(jnp.float32)),
                          0.0)
    scores = jnp.einsum('bnihd,bnjhd->bnhij', q, k) * decay_mat
    o_inner = jnp.einsum('bnhij,bnjhe->bnihe', scores, v)
    q_decay = jnp.exp(log_gamma[:, None] * (idx + 1).astype(jnp.float32))
    k_decay = jnp.exp(log_gamma[:, None] * (C - 1 - idx).astype(jnp.float32))
    chunk_decay = jnp.exp(log_gamma * C)[None, :, None, None]
    kv_chunk = jnp.einsum('bnjhd,hj,bnjhe->bnhde', k, k_decay, v)

    def step(state, kv_n):
        return state * chunk_decay + kv_n, state

    init = jnp.zeros((B_, H, dk, dv), jnp.float32)
    _, prev_states = lax.scan(step, init, jnp.moveaxis(kv_chunk, 1, 0))
    prev_states = jnp.moveaxis(prev_states, 0, 1)
    o_cross = jnp.einsum('bnihd,hi,bnhde->bnihe', q, q_decay, prev_states)
    o = o_inner + o_cross
    o = o * lax.rsqrt(jnp.mean(o * o, axis=-1, keepdims=True) + RMS_EPS)
    o = o.reshape(B_, T, H * dv)
    y = jax.nn.silu(g.astype(jnp.float32)) * o
    return y.astype(h.dtype) @ w_o

def squared_relu_mlp(h, w_up, w_down):
    a = jax.nn.relu(h @ w_up)
    return (a * a) @ w_down

def second_inputs(seed: int = 0) -> dict:
    key = jax.random.key(seed)
    ks = jax.random.split(key, 16)

    def dense(k, shape):
        return jax.random.normal(k, shape, jnp.float32) * (shape[-2] ** -0.5)

    def gain(k, shape):
        return 1.0 + 0.02 * jax.random.normal(k, shape, jnp.float32)

    swa_qkv_dim = (SWA_HEADS + 2 * SWA_KV_HEADS) * SWA_HEAD_DIM
    ret_in_dim = 2 * RET_HEADS * RET_QK_DIM + 2 * RET_HEADS * RET_V_DIM
    return {
        "x": jax.random.normal(ks[0], (BATCH, SEQ, D_MODEL), jnp.float32),
        "attn_norm": gain(ks[1], (DEPTH_2, D_MODEL)),
        "mlp_norm": gain(ks[2], (DEPTH_2, D_MODEL)),
        "final_norm": gain(ks[3], (D_MODEL,)),
        "swa_w_qkv": dense(ks[4], (N_A, D_MODEL, swa_qkv_dim)),
        "swa_sinks": 0.5 * jax.random.normal(ks[5], (N_A, SWA_HEADS), jnp.float32),
        "swa_w_o": dense(ks[6], (N_A, SWA_HEADS * SWA_HEAD_DIM, D_MODEL)),
        "sb_w_qkv": dense(ks[7], (N_B, D_MODEL, 3 * SB_HEADS * SB_HEAD_DIM)),
        "sb_w_o": dense(ks[8], (N_B, SB_HEADS * SB_HEAD_DIM, D_MODEL)),
        "ret_w_in": dense(ks[9], (N_C, D_MODEL, ret_in_dim)),
        "ret_w_o": dense(ks[10], (N_C, RET_HEADS * RET_V_DIM, D_MODEL)),
        "mlp_w_up": dense(ks[11], (DEPTH_2, D_MODEL, D_FF)),
        "mlp_w_down": dense(ks[12], (DEPTH_2, D_FF, D_MODEL)),
    }

def second_block(x, attn_norm, mlp_norm, final_norm, swa_w_qkv, swa_sinks, swa_w_o,
              sb_w_qkv, sb_w_o, ret_w_in, ret_w_o, mlp_w_up, mlp_w_down):
    h = x
    for i in range(DEPTH_2):
        kind, j = i % N_MIXERS, i // N_MIXERS
        u = rms_norm_2(h, attn_norm[i])
        if kind == 0:
            mix = swa_mixer(u, swa_w_qkv[j], swa_sinks[j], swa_w_o[j])
        elif kind == 1:
            mix = stick_breaking_mixer(u, sb_w_qkv[j], sb_w_o[j])
        else:
            mix = retention_mixer(u, ret_w_in[j], ret_w_o[j])
        h = h + mix
        h = h + squared_relu_mlp(rms_norm_2(h, mlp_norm[i]), mlp_w_up[i], mlp_w_down[i])
    return rms_norm_2(h, final_norm)


def setup_inputs(seed=0):
    out = dict(first_inputs(seed))
    for name, value in second_inputs(seed + 1).items():
        if name != "x":
            out[name + "_2"] = value
    return out


def reference(
    x, p, w_in_even, conv_a_w, conv_b_w, a_log, dt_bias, gdn_norm_g, w_out_even, w_in_odd,
    lower_bounds, hgrn_norm_g, w_out_odd, ln_g, ln_b, w_pl, w_pl_gate, attn_norm_2, mlp_norm_2,
    final_norm_2, swa_w_qkv_2, swa_sinks_2, swa_w_o_2, sb_w_qkv_2, sb_w_o_2, ret_w_in_2,
    ret_w_o_2, mlp_w_up_2, mlp_w_down_2,
):
    x = first_block(
        x, p, w_in_even, conv_a_w, conv_b_w, a_log, dt_bias, gdn_norm_g, w_out_even, w_in_odd,
        lower_bounds, hgrn_norm_g, w_out_odd, ln_g, ln_b, w_pl, w_pl_gate,
    )
    return second_block(
        x, attn_norm_2, mlp_norm_2, final_norm_2, swa_w_qkv_2, swa_sinks_2, swa_w_o_2,
        sb_w_qkv_2, sb_w_o_2, ret_w_in_2, ret_w_o_2, mlp_w_up_2, mlp_w_down_2,
    )


_drawn_inputs = setup_inputs


def setup_inputs(seed=0):
    import zlib

    import numpy as np

    out = dict(_drawn_inputs(seed))
    spreads = {}
    factors = {'gdn_norm_g': 8.0,
     'lower_bounds': 8.0,
     'hgrn_norm_g': 8.0,
     'attn_norm_2': 6.432,
     'mlp_norm_2': 9.416,
     'final_norm_2': 8.113,
     'swa_sinks_2': 8.0}
    for name, (base, spread) in spreads.items():
        noise = np.random.default_rng([zlib.crc32(name.encode()), seed]).standard_normal(out[name].shape)
        drawn = base * np.exp(spread * noise) if base else spread * noise
        out[name] = __import__('jax').numpy.asarray(drawn.astype(out[name].dtype))
    for name, factor in factors.items():
        out[name] = (out[name] * factor).astype(out[name].dtype)
    return out
```

```python
from contextlib import ExitStack

import concourse.bass as bass
from concourse import mybir

F32 = mybir.dt.float32
F32R = mybir.dt.float32r
I32 = mybir.dt.int32
ALU = mybir.AluOpType
ACT = mybir.ActivationFunctionType
AX_X = mybir.AxisListType.X

P = 128
T = 256
NT = T // P
D = 1024
KT = D // P
COLS = 512
RAWK = 4
SPLK = 2
NRAW = 3
NSPL = 6
AHEAD = 4
GH = 8
HH = 16
AH = 16
AD = 64
ALPHA = 4.0 ** 0.25
EPS = 1e-5
RMS_EPS = 1e-6
LEVELS = [1, 2, 4, 8, 16, 32, 64]
STACK_A = 96
CONV_A, LB, LNG, LNB, ATTN, MLPN, GDNG, HGRNG, STACK_B = 0, 24, 56, 72, 88, 96, 104, 105, 106

C_ID, C_UPTO, C_AFTER, C_ONES = 0, P, 2 * P, 3 * P
C_NEG = 4 * P
C_NEG1T = C_NEG + len(LEVELS) * P
C_PICK = C_NEG1T + P
C_DIST = C_PICK + len(LEVELS) * P // 2
C_ALL = C_DIST + 2 * P
EXP_TABLES = "exp_and_others"
LOG_TABLES = "natural_log_exp_and_others"


class Count:

    def __init__(self, sem):
        self.sem = sem
        self.n = 0


def chunk_list():
    out = [("qkvz", h, 0) for h in range(GH)] + [("hcbz", j, 0) for j in range(KT)]
    out += [("out_even", c, g) for g in range(2) for c in range(2)]
    out += [("pl", 0, 0)] + [("gate", c, 0) for c in range(2)]
    out += [("qfiz", h, 0) for h in range(HH)]
    out += [("out_odd", c, g) for g in range(2) for c in range(2)]
    out += [("pl", 1, 0)] + [("gate", 2 + c, 0) for c in range(2)]
    out += [("q_att", c, 0) for c in range(2)] + [("kv_att", 0, 0)] + [("o_att", c, 0) for c in range(2)]
    out += [("up", c, 0) for c in range(8)] + [("down", c, g) for g in range(4) for c in range(2)]
    return out


CHUNKS = chunk_list()
FIRST_SPLIT = {}
_n = 0
for _c in CHUNKS:
    FIRST_SPLIT[_c] = _n
    _n += 2 if _c[0] == "pl" else 4
SPLITS = _n
GROUPS = [("x_t", 0), ("x_t", 1)] + [("qkvz", h) for h in range(GH)] + [("hcbz", j) for j in range(KT)]
GROUPS += [("out_even", 0), ("out_even", 1), ("ln_t", 0), ("ln_t", 1), ("gate", 0), ("gate", 1), ("x2_t", 0), ("x2_t", 1)]
GROUPS += [("qfiz", h) for h in range(HH)]
GROUPS += [("out_odd", 0), ("out_odd", 1), ("ln_t", 2), ("ln_t", 3), ("gate", 2), ("gate", 3), ("att_t", 0), ("att_t", 1)]
GROUPS += [("q_att", 0), ("q_att", 1), ("kv_att", 0)] + [("score", t) for t in range(8)]
GROUPS += [("o_att", 0), ("o_att", 1), ("mlp_t", 0), ("mlp_t", 1)] + [("up", c) for c in range(8)] + [("down", 0), ("down", 1)]
GROUP = {g: i for i, g in enumerate(GROUPS)}
UNITS_DONE = {(n, i): u + 4 for (n, i, _), u in FIRST_SPLIT.items() if n != "pl"}
TURNED = {g: i + 1 for i, g in enumerate(g for g in GROUPS if g not in UNITS_DONE)}

GSTEPS = 21
PE_STEPS = [(s, g) for s in range(GSTEPS) for g in range(2) if (s, g) not in ((17, 1), (18, 0))]
DVE_STEPS = [(s, g) for s, g in PE_STEPS if s != 19]


def pe_step(half, s, g):
    return half * len(PE_STEPS) + PE_STEPS.index((s, g)) + 1


def dve_step(half, s, g):
    return half * len(DVE_STEPS) + DVE_STEPS.index((s, g)) + 1


def build(nc, a, consts, out):
    with ExitStack() as ctx:
        def sem(name):
            return ctx.enter_context(nc.semaphore(name))

        def sb(name, shape, dt=F32, stack=ctx):
            return stack.enter_context(nc.sbuf_tensor(name, shape, dt))

        raw = sb("raw", [P, NRAW, RAWK * COLS])
        whi = sb("whi", [P, NSPL, SPLK * COLS], F32R)
        wlo = sb("wlo", [P, NSPL, SPLK * COLS], F32R)
        con = sb("con", [P, C_ALL])
        colA = sb("colA", [P, STACK_A])
        colB = sb("colB", [P, STACK_B])
        xtok = sb("xtok", [P, NT, D])
        x_hi = sb("x_hi", [P, KT, T], F32R)
        x_lo = sb("x_lo", [P, KT, T], F32R)
        ya_hi = sb("ya_hi", [P, KT, T], F32R)
        ya_lo = sb("ya_lo", [P, KT, T], F32R)
        with ExitStack() as ph:
            qT = sb("qT", [P, GH, T], stack=ph)
            kT = sb("kT", [P, GH, T], stack=ph)
        with ExitStack() as ph:
            lg = sb("lg", [P, 2, 6 * P], stack=ph)
            pt = sb("pt", [P, 2, 6 * P], stack=ph)
        yb_hi = sb("yb_hi", [P, GH, T], F32R)
        yb_lo = sb("yb_lo", [P, GH, T], F32R)

        ident = con[:, C_ID:C_ID + P]
        upto = con[:, C_UPTO:C_UPTO + P]
        after = con[:, C_AFTER:C_AFTER + P]
        ones = con[:, C_ONES:C_ONES + P]
        neg = {s: con[:, C_NEG + i * P:C_NEG + (i + 1) * P] for i, s in enumerate(LEVELS)}
        neg1t = con[:, C_NEG1T:C_NEG1T + P]
        pick = {s: con[:, C_PICK + 64 * i:C_PICK + 64 * (i + 1)].bitcast(I32) for i, s in enumerate(LEVELS)}
        ndist = con[:, C_DIST:C_DIST + 2 * P]

        with ExitStack() as ph:
            vT = sb("vT", [P, GH, T], stack=ph)
            szb = sb("szb", [P, GH, T], stack=ph)
            pad = sb("pad", [P, 3, T + 4], stack=ph)
            thz = sb("thz", [P, T], stack=ph)
            hs = sb("hs", [P, T], stack=ph)
            upad = sb("upad", [P, T + 2], stack=ph)
            yf = sb("yf", [P, T], stack=ph)
            tail_w = sb("tail_w", [P, KT, 16], stack=ph)
            tail_hi = sb("tail_hi", [P, KT, 16], F32R, stack=ph)
            tail_lo = sb("tail_lo", [P, KT, 16], F32R, stack=ph)
            gate_rows = sb("gate_rows", [P, 2, GH], stack=ph)
            gt = sb("gt", [P, 8, NT, GH], stack=ph)
            GAF = sb("GAF", [P, 2, 4 * P], stack=ph)
            EL = sb("EL", [P, 2, 4 * P], stack=ph)
            AT = sb("AT", [P, 2, 4 * P], stack=ph)
            LT = sb("LT", [P, 2, 4 * P], stack=ph)
            XN = sb("XN", [P, 2, 4 * P], stack=ph)
            XT = sb("XT", [P, 2, 4 * P], stack=ph)
            KX = sb("KX", [P, 2, 4 * P], stack=ph)
            VB = sb("VB", [P, 2, 4 * P], stack=ph)
            QD = sb("QD", [P, 2, 4 * P], stack=ph)
            cv = AT[:, :, :].rearrange("p g c -> p (g c)")[:, 0:3 * T]
            th = KX[:, :, :].rearrange("p g c -> p (g c)")[:, 0:3 * T]
            xf0 = VB
            stA = GAF[0:STACK_A, 0, 0:P]
            stB = GAF[0:STACK_B, 1, 0:P]
        with ExitStack() as ph:
            qfth = sb("qfth", [P, 2, 2 * T], stack=ph)
            zth = sb("zth", [P, 2, T], stack=ph)
            vfm = sb("vfm", [P, 2, 2, T], stack=ph)
            q0 = sb("q0", [P, 2, 2 * T], stack=ph)
            QS = sb("QS", [P, 2, 2 * T], stack=ph)
            KS = sb("KS", [P, 2, 2 * T], stack=ph)
            F0 = sb("F0", [P, 2, 2 * T], stack=ph)
            F1 = sb("F1", [P, 2 * T], stack=ph)
            AA = sb("AA", [P, 2, 4 * P], stack=ph)
            CR = sb("CR", [P, 2, 2 * P], stack=ph)
            vtok = sb("vtok", [P, 2, 4 * P], stack=ph)
            szo = sb("szo", [P, 3, 2 * T], stack=ph)
            sqo = sb("sqo", [P, 2 * T], stack=ph)
            rso = sb("rso", [P, 2 * T], stack=ph)
            yo = sb("yo", [P, 2 * T], stack=ph)
            lbc = sb("lbc", [P, 6, HH], stack=ph)
        zt = sb("zt", [P, NT, D])
        gb = sb("gb", [P, 2, D])
        eg = sb("eg", [P, 2, COLS])
        xf = sb("xf", [P, 2, 2 * T])
        ptk = sb("ptk", [P, NT, T])
        pf = sb("pf", [P, NT, T])
        p_hi = sb("p_hi", [P, NT, T], F32R)
        p_lo = sb("p_lo", [P, NT, T], F32R)
        stats = sb("stats", [P, NT, 2, 6])
        mv = sb("mv", [P, NT, 4])
        rl = zt
        with ExitStack() as ph:
            qa = sb("qa", [P, KT, T], stack=ph)
            ka = sb("ka", [P, 2, T], stack=ph)
            va = sb("va", [P, 2, P], stack=ph)
            bias = sb("bias", [P, AH, 2 * P], stack=ph)
            sink_row = sb("sink_row", [P, AH], stack=ph)
            st_att = sb("st_att", [P, 2, 4, 4], stack=ph)
            ysw = sb("ysw", [P, 2, T], stack=ph)
        ac_hi = sb("ac_hi", [P, 16, T], F32R)
        ac_lo = sb("ac_lo", [P, 16, T], F32R)

        def act_tiles(c):
            hi, lo, b = ((ya_hi, ya_lo, 0), (yb_hi, yb_lo, 8))[c // 2] if c < 4 else (ac_hi, ac_lo, 16)
            return hi[:, 4 * c - b:4 * c - b + 4, :], lo[:, 4 * c - b:4 * c - b + 4, :]

        DB = [[ctx.enter_context(nc.psum_tensor(f"dense{i}{j}", [P, 512], F32)) for j in range(2)] for i in range(2)]
        SB = [ctx.enter_context(nc.psum_tensor(f"bank{i}", [P, 512], F32)) for i in range(4)]

        raw_ready = [sem(f"raw_ready{i}") for i in range(NRAW)]
        pair_free = [sem("pair_free0"), sem("pair_free1")]
        hi_done = sem("hi_done")
        lo_done = sem("lo_done")
        split_used = sem("split_used")
        turned = sem("turned")
        x_loaded = sem("x_loaded")
        consts_loaded = sem("consts_loaded")
        stacks_loaded = sem("stacks_loaded")
        tail_loaded = sem("tail_loaded")
        rows_loaded = sem("rows_loaded")
        norm_rows = sem("norm_rows")
        p_loaded = sem("p_loaded")
        stored = sem("stored")
        stack_t = sem("stack_t")
        cols_taken = sem("cols_taken")
        tail_split = sem("tail_split")
        tail_low = sem("tail_low")
        tail_out = sem("tail_out")
        tail_copied = sem("tail_copied")
        gates_tanh = sem("gates_tanh")
        gates_abs = sem("gates_abs")
        gates_log = sem("gates_log")
        gates_ready = sem("gates_ready")
        gate_sums = sem("gate_sums")
        gate_exp = sem("gate_exp")
        xf_done = sem("xf_done")
        xhi_done = sem("xhi_done")
        x_ready = sem("x_ready")
        p_t = sem("p_t")
        pf_done = sem("pf_done")
        p_hi_done = sem("p_hi_done")
        p_ready = sem("p_ready")
        conv_copied = sem("conv_copied")
        conv_done = sem("conv_done")
        conv_tanh = sem("conv_tanh")
        z_tanh = sem("z_tanh")
        qkv_done = sem("qkv_done")
        h_copied = sem("h_copied")
        ya_done = sem("ya_done")
        ya_hi_done = sem("ya_hi_done")
        ya_ready = sem("ya_ready")
        norm_sq = sem("norm_sq")
        norm_sum = sem("norm_sum")
        norm_rs = sem("norm_rs")
        norm_done = sem("norm_done")
        gdn_gates = sem("gdn_gates")
        gdn_products = sem("gdn_products")
        gdn_vector = sem("gdn_vector")
        gdn_exp = sem("gdn_exp")
        gdn_squares = sem("gdn_squares")
        gdn_rstd = sem("gdn_rstd")
        gdn_gated = sem("gdn_gated")
        gdn_hi = sem("gdn_hi")
        gdn_ready = sem("gdn_ready")
        r_done = sem("r_done")
        mean_done = sem("mean_done")
        rstd_done = sem("rstd_done")
        squares_done = sem("squares_done")
        z_ready = sem("z_ready")
        gate_tanh = sem("gate_tanh")
        x2_done = sem("x2_done")
        lb_diff = sem("lb_diff")
        lb_exp = sem("lb_exp")
        lb_done = sem("lb_done")
        hg_act = sem("hg_act")
        hg_gated = sem("hg_gated")
        hg_level_mm = sem("hg_level_mm")
        hg_level = sem("hg_level")
        hg_cross_mm = sem("hg_cross_mm")
        hg_cross = sem("hg_cross")
        hg_vt = sem("hg_vt")
        hg_vt_taken = sem("hg_vt_taken")
        hg_o = sem("hg_o")
        hg_sq = sem("hg_sq")
        hg_sum = sem("hg_sum")
        hg_rs = sem("hg_rs")
        hg_y = sem("hg_y")
        hg_hi = sem("hg_hi")
        hg_ready = sem("hg_ready")
        att_in = sem("att_in")
        bias_done = sem("bias_done")
        att_neg = sem("att_neg")
        att_exp = sem("att_exp")
        att_prob = sem("att_prob")
        att_t = sem("att_t")
        att_pt0 = sem("att_pt0")
        att_pt1 = sem("att_pt1")
        att_o = sem("att_o")
        att_of = sem("att_of")
        att_hi = sem("att_hi")
        att_ready = sem("att_ready")
        relu_done = sem("relu_done")
        squared = sem("squared")
        a_hi_done = sem("a_hi_done")
        a_ready = sem("a_ready")
        final_done = sem("final_done")

        vec_chain, act_chain = sem("vec_chain"), sem("act_chain")

        def pair_of(name, i):
            return DB[GROUP[(name, i)] % 2]

        def unit_slot(u):
            return raw[:, (u // 2) % NRAW, (u % 2) * SPLK * COLS:(u % 2 + 1) * SPLK * COLS]

        def weights(c, half):
            name, i, g = c
            k0 = (g * KT + half * RAWK) * P

            def rows(w, n=RAWK):
                return w[k0:k0 + n * P, :].rearrange("(k p) c -> p k c", p=P)

            if name == "qkvz":
                return rows(a["w_in_even"][0][:, 4 * D:8 * D]).rearrange("p k (s c) -> p k s c", s=4)[:, :, :, i * P:(i + 1) * P]
            if name == "hcbz":
                return rows(a["w_in_even"][0][:, 0:4 * D]).rearrange("p k (s c) -> p k s c", s=4)[:, :, :, i * P:(i + 1) * P]
            if name == "qfiz":
                return rows(a["w_in_odd"][0]).rearrange("p k (s c) -> p k s c", s=4)[:, :, :, i * P:(i + 1) * P]
            if name == "pl":
                return rows(a["w_pl"][i], 2)
            tensor, layer, col = {"out_even": ("w_out_even", 0, i), "out_odd": ("w_out_odd", 0, i), "gate": ("w_pl_gate", i // 2, i % 2),
                                  "q_att": ("swa_w_qkv_2", 0, i), "o_att": ("swa_w_o_2", 0, i),
                                  "up": ("mlp_w_up_2", 0, i), "down": ("mlp_w_down_2", 0, i)}[name]
            w = a[tensor][layer]
            return rows(w[:, col * COLS:(col + 1) * COLS])

        ready_at = []
        total = [0] * NRAW
        for c in CHUNKS:
            for half in range(1 if c[0] == "pl" else 2):
                slot = len(ready_at) % NRAW
                total[slot] += 16 * {"kv_att": 6, "qkvz": 4, "hcbz": 4, "qfiz": 4}.get(c[0], 1)
                ready_at.append(total[slot])

        block = ctx.enter_context(nc.Block())

        @block.sync
        def _(sp):
            n = 0
            for c in CHUNKS:
                for half in range(1 if c[0] == "pl" else 2):
                    slot = n % NRAW
                    if n >= NRAW:
                        sp.wait_ge(lo_done, 2 * (n - NRAW + 1))
                    dst = raw[:, slot, :]
                    if c[0] == "kv_att":
                        w = a["swa_w_qkv_2"][0][half * RAWK * P:(half + 1) * RAWK * P, AH * AD:AH * AD + 2 * P]
                        w = w.rearrange("(k p) c -> p k c", p=P)
                        d = dst.rearrange("p (k c) -> p k c", k=RAWK)
                        for j in range(4):
                            sp.dma_start(d[:, :, j * AD:(j + 1) * AD], w[:, :, (j // 2) * AD:(j // 2 + 1) * AD]).then_inc(raw_ready[slot], 16)
                        for r in range(2):
                            sp.dma_start(d[:, :, (2 + r) * P:(3 + r) * P], w[:, :, P:2 * P]).then_inc(raw_ready[slot], 16)
                    elif c[0] in ("qkvz", "hcbz", "qfiz"):
                        d, w = dst.rearrange("p (k s c) -> p k s c", k=RAWK, s=4), weights(c, half)
                        for k in range(RAWK):
                            sp.dma_start(d[:, k], w[:, k]).then_inc(raw_ready[slot], 16)
                    else:
                        w = weights(c, half)
                        sp.dma_start(dst.rearrange("p (k c) -> p k c", k=w.shape[1]), w).then_inc(raw_ready[slot], 16)
                    n += 1

        @block.gpsimd
        def _(pool):
            for u in range(SPLITS):
                pool.wait_ge(hi_done, u + 1)
                if u >= NSPL:
                    pool.wait_ge(split_used, u - NSPL + 1)
                pool.tensor_tensor(wlo[:, u % NSPL, :], unit_slot(u), whi[:, u % NSPL, :].bitcast(F32),
                                   ALU.subtract).then_inc(lo_done, 1)

        @block.tensor
        def _(pe):
            at = {"unit": 0}

            def group_start(name, i):
                o = GROUP[(name, i)]
                if o >= 2:
                    pe.wait_ge(pair_free[o % 2], o // 2)

            def three(out_, lw, rw, start, stop, l_cols=None):
                (lh, ll), (rh, rl_) = lw, rw
                pe.matmul(out_, lh, rh, start=start, stop=False, skip_group_check=True)
                pe.matmul(out_, lh, rl_, start=False, stop=False, skip_group_check=True)
                return pe.matmul(out_, ll, rh, start=False, stop=stop, skip_group_check=True)

            def unit_ready():
                u = at["unit"]
                pe.wait_ge(lo_done, u + 1)
                at["unit"] += 1
                slot = u % NSPL
                return (whi[:, slot, :].rearrange("p (k c) -> p k c", k=SPLK), wlo[:, slot, :].rearrange("p (k c) -> p k c", k=SPLK))

            def feature_unit(name, i, q, xh, xl, tiles=4):
                if q == 0:
                    group_start(name, i)
                wh, wl = unit_ready()
                bank = pair_of(name, i)
                for kk in range(SPLK):
                    k = q * SPLK + kk
                    for t in range(tiles):
                        cols = slice(t * P, (t + 1) * P)
                        last = three(bank[t // 2][:, (t % 2) * T:(t % 2 + 1) * T], (wh[:, kk, cols], wl[:, kk, cols]),
                                     (xh[:, k, :], xl[:, k, :]), start=(k == 0 and t % 2 == 0), stop=(k == KT - 1))
                return last

            def token_unit(name, i, q, xh, xl, start, stop):
                wh, wl = unit_ready()
                bank = pair_of(name, i)
                for kk in range(SPLK):
                    k = q * SPLK + kk
                    for t in range(NT):
                        tok = slice(t * P, (t + 1) * P)
                        last = three(bank[t][:, :], (xh[:, k, tok], xl[:, k, tok]), (wh[:, kk, :], wl[:, kk, :]),
                                     start=start and kk == 0, stop=stop and kk == SPLK - 1)
                return last

            def dense_feature(name, i, q, xh, xl):
                feature_unit(name, i, q, xh, xl).then_inc(split_used, 1)

            def transposes(name, first, src, source_ready, counts):
                for c in range(2):
                    pe.wait_ge(source_ready, counts[c])
                    group_start(name, first + c)
                    bank = pair_of(name, first + c)
                    for b in range(2):
                        for j in range(2):
                            for t in range(NT):
                                k = 4 * c + 2 * b + j
                                last = pe.transpose(bank[b][:, j * T + t * P:j * T + (t + 1) * P], src[:, t, k * P:(k + 1) * P], ident)
                    last.then_inc(turned, 1)

            def layer_tail(layer):
                pe.wait_ge(p_ready, layer + 1)
                for k in range(2):
                    wh, wl = unit_ready()
                    for t in range(NT):
                        tok = slice(t * P, (t + 1) * P)
                        for c in range(2):
                            cols = slice(c * COLS, (c + 1) * COLS)
                            w = [x[:, :, :].rearrange("p k c -> p (k c)")[:, cols] for x in (wh, wl)]
                            last = three(SB[2 * t + c][:, :], (p_hi[:, k, tok], p_lo[:, k, tok]), w, start=(k == 0), stop=(k == 1))
                    last.then_inc(split_used, 1)
                transposes("ln_t", 2 * layer, zt, z_ready, [2 * layer + 2] * 2)
                for c in range(2):
                    group_start("gate", 2 * layer + c)
                    for q in range(4):
                        pe.wait_ge(x_ready, 4 + 8 * layer + q + 1)
                        token_unit("gate", 2 * layer + c, q, ya_hi, ya_lo, q == 0, q == 3).then_inc(split_used, 1)

            def p_transposes(layer):
                pe.wait_ge(p_loaded, 16 * (layer + 1))
                for k in range(2):
                    for t in range(NT):
                        last = pe.transpose(SB[0][:, k * T + t * P:k * T + (t + 1) * P], ptk[:, t, k * P:(k + 1) * P], ident)
                last.then_inc(p_t, 1)

            pe.wait_ge(consts_loaded, 16)
            pe.wait_ge(stacks_loaded, 144)
            pe.transpose(SB[0][:, 0:STACK_A], stA, ident[0:STACK_A, 0:STACK_A])
            pe.transpose(SB[0][:, P:P + STACK_B], stB, ident[0:STACK_B, 0:STACK_B]).then_inc(stack_t, 1)
            transposes("x_t", 0, xtok, x_loaded, [32, 32])

            def tail():
                pe.wait_ge(tail_low, 1)
                for t in range(NT):
                    tok = slice(t * P, (t + 1) * P)
                    for k in range(KT):
                        last = three(SB[1][:, 16 * t:16 * t + 16], (x_hi[:, k, tok], x_lo[:, k, tok]), (tail_hi[:, k, :], tail_lo[:, k, :]),
                                     start=(k == 0), stop=(k == KT - 1))
                last.then_inc(tail_out, 1)

            for h in range(GH):
                for q in range(4):
                    if h == 0:
                        pe.wait_ge(x_ready, q + 1)
                    dense_feature("qkvz", h, q, x_hi, x_lo)
                if h == 0:
                    tail()
                if h == 2:
                    pe.wait_ge(gates_ready, 1)
                    pe.wait_ge(cols_taken, 1)
                    pe.matmul(SB[0][:, 0:GH], after, gt[:, 5, 0, :], start=True, stop=True)
                    pe.matmul(SB[0][:, GH:2 * GH], upto, gt[:, 5, 1, :], start=True, stop=True).then_inc(gate_sums, 1)

            def unit(g_buf, u):
                return g_buf[:, u * P:(u + 1) * P]

            def even_odd(ap, s, which):
                return ap.rearrange("p (m t r) -> p m t r", t=2, r=s)[:, :, which, :]

            def norm_products(half):
                for n in range(4):
                    pe.wait_ge(norm_sq, 4 * half + n + 1)
                    if half == 0 and n == 0:
                        pe.wait_ge(gate_exp, 1)
                    if half == 1 and n == 0:
                        pe.wait_ge(gdn_vector, dve_step(0, 20, 1))
                    src = (EL if n < 2 else LT)[:, n % 2, :]
                    pe.matmul(SB[n][:, :], ones, src, start=True, stop=True).then_inc(norm_sum, 1)

            def gdn(half, s):
                for g in range(2):
                    if (s, g) not in PE_STEPS:
                        continue
                    A, B = SB[2 * g], SB[2 * g + 1]
                    tok = slice(g * P, (g + 1) * P)
                    heads = [4 * half + u for u in range(4)]
                    if s == 0:
                        pe.wait_ge(gdn_gates, half + 1)
                        pe.wait_ge(norm_rs, 4 * half + 4)
                    elif s == 1:
                        pe.wait_ge(norm_done, 4 * half + 4)
                        pe.wait_ge(gdn_vector, dve_step(half, 0, g))
                    elif s < 17:
                        pe.wait_ge(gdn_vector, dve_step(half, s - 1, g))
                    elif s == 17:
                        pe.wait_ge(gdn_vector, dve_step(half, 16, 0))
                    elif s == 18:
                        pe.wait_ge(gdn_vector, dve_step(half, 17, 0))
                    elif s == 19:
                        pe.wait_ge(gdn_vector, dve_step(half, 18, 1))
                    else:
                        pe.wait_ge(gdn_squares, 2 * half + g + 1)
                    for u, h in enumerate(heads):
                        o = slice(u * P, (u + 1) * P)
                        if s == 0:
                            pe.matmul(A[:, o], upto, unit(GAF[:, g, :], u), start=True, stop=True)
                            last = pe.matmul(B[:, o], unit(GAF[:, g, :], u), upto, start=True, stop=True)
                        elif s == 1:
                            pe.matmul(A[:, o], kT[:, h, tok], kT[:, h, tok], start=True, stop=True)
                            last = pe.matmul(B[:, o], kT[:, h, tok], qT[:, h, tok], start=True, stop=True)
                        elif s == 2:
                            last = pe.transpose(A[:, o], unit(EL[:, g, :], u), ident)
                            if g == 1:
                                last = pe.matmul(B[:, o], gt[:, 5, 1, h:h + 1].broadcast_to([P, P]), upto, start=True, stop=True)
                        elif s == 3:
                            pe.transpose(A[:, o], kT[:, h, tok], ident)
                            last = pe.transpose(B[:, o], vT[:, h, tok], ident)
                        elif s < 16 and s % 2 == 0:
                            last = pe.matmul(A[:, o], unit(LT[:, g, :], u), unit(XN[:, g, :], u), start=True, stop=True)
                        elif s < 16:
                            lv = LEVELS[(s - 5) // 2 + 1]
                            if s != 15:
                                pe.matmul(B[:, u * 64:(u + 1) * 64], unit(XT[:, g, :], u), even_odd(unit(EL[:, g, :], u), lv, 0), start=True, stop=True)
                            last = pe.matmul(B[:, 256 + u * 64:256 + (u + 1) * 64], unit(EL[:, g, :], u), even_odd(unit(XT[:, g, :], u), lv, 1),
                                             start=True, stop=True)
                        elif s == 16 and g == 0:
                            last = pe.matmul(A[:, o], unit(XT[:, 0, :], u), unit(VB[:, 0, :], u), start=True, stop=True)
                        elif s == 16:
                            last = pe.matmul(A[:, o], unit(KX[:, 1, :], u), unit(XT[:, 1, :], u), start=True, stop=True)
                        elif s == 17:
                            last = pe.matmul(B[:, o], unit(KX[:, 0, :], u), unit(XN[:, 0, :], u), start=True, stop=True)
                        elif s == 18:
                            pe.matmul(A[:, o], unit(XT[:, 1, :], u), unit(VB[:, 1, :], u), start=True, stop=False)
                            last = pe.matmul(A[:, o], unit(LT[:, 1, :], u), unit(LT[:, 0, :], u), start=False, stop=True)
                    if s == 19:
                        for j in range(2):
                            u = 2 * g + j
                            pe.matmul(A[:, j * T:j * T + P], unit(XN[:, 0, :], u), unit(AT[:, 0, :], u), start=True, stop=True)
                            pe.matmul(A[:, j * T + P:(j + 1) * T], unit(LT[:, 0, :], u), unit(QD[:, 1, :], u), start=True, stop=False)
                            last = pe.matmul(A[:, j * T + P:(j + 1) * T], unit(XN[:, 1, :], u), unit(AT[:, 1, :], u), start=False, stop=True)
                    if s == 20:
                        last = pe.matmul(B[:, :], ones, EL[:, g, :], start=True, stop=True)
                    last.then_inc(gdn_products, 1)

            def out_unit(name, n):
                g, c, q = n // 8, n // 4 % 2, n % 4
                if g == 0 and q == 0:
                    group_start(name, c)
                xh, xl = ((ya_hi, ya_lo), (yb_hi, yb_lo))[g]
                if name == "out_even":
                    pe.wait_ge(ya_ready if g == 0 else gdn_ready, 2 * q + 2 if g == 0 else q + 1)
                else:
                    pe.wait_ge(hg_ready, 4 * g + q + 1)
                token_unit(name, c, q, xh, xl, g == 0 and q == 0, g == 1 and q == 3).then_inc(split_used, 1)

            slot = 0
            for half in range(2):
                norm_products(half)
                for s in range(GSTEPS):
                    if slot < 32:
                        dense_feature("hcbz", slot // 4, slot % 4, x_hi, x_lo)
                    else:
                        out_unit("out_even", slot - 32)
                    gdn(half, s)
                    slot += 1
            for n in range(slot - 32, 16):
                if n == 12:
                    p_transposes(0)
                out_unit("out_even", n)
            layer_tail(0)
            transposes("x2_t", 0, xtok, x2_done, [1, 2])

            def hg_unit(buf, par, i, t):
                return buf[:, par, i * T + t * P:i * T + (t + 1) * P]

            for it in range(HH // 2 + 2):
                L, C = it - 1, it - 2
                pl_, pc = L % 2, C % 2
                for k in range(8):
                    if it < HH // 2:
                        if it == 0:
                            pe.wait_ge(x_ready, 8 + k % 4 + 1)
                        dense_feature("qfiz", 2 * it + k // 4, k % 4, x_hi, x_lo)
                    else:
                        out_unit("out_odd", (it - HH // 2) * 8 + k)
                    if k == 0 and 0 <= C < HH // 2:
                        pe.wait_ge(hg_level, 7 * C + 7)
                        for i in range(2):
                            last = pe.matmul(SB[0][:, i * P:(i + 1) * P], hg_unit(KS, pc, i, 0), hg_unit(QS, pc, i, 1), start=True, stop=True)
                        last.then_inc(hg_cross_mm, 1)
                    if k == 0 and 0 <= L < HH // 2:
                        pe.wait_ge(hg_act, 2 * L + 2)
                        if C > 0:
                            pe.wait_ge(hg_rs, C)
                        for i in range(2):
                            for t in range(NT):
                                last = pe.transpose(SB[2][:, (2 * i + t) * P:(2 * i + t + 1) * P], vfm[:, pl_, i, t * P:(t + 1) * P], ident)
                        last.then_inc(hg_vt, 1)
                    if k >= 1 and 0 <= L < HH // 2:
                        if k == 1:
                            pe.wait_ge(hg_gated, 2 * L + 2)
                            pe.wait_ge(hg_cross, C + 1)
                            if 7 * L > 0:
                                pe.wait_ge(hg_level, 7 * L)
                        else:
                            pe.wait_ge(hg_level, 7 * L + k - 1)
                        s = LEVELS[k - 1]
                        for i in range(2):
                            for t in range(NT):
                                u = 2 * i + t
                                if k == 1:
                                    pe.matmul(SB[0][:, u * P:(u + 1) * P], hg_unit(KS, pl_, i, t), hg_unit(q0, pl_, i, t), start=True, stop=True)
                                last = pe.matmul(SB[k % 2][:, u * 64:(u + 1) * 64], hg_unit(KS, pl_, i, t), even_odd(hg_unit(QS, pl_, i, t), s, 1),
                                                 start=True, stop=True)
                        last.then_inc(hg_level_mm, 1)
                    if k == 1 and 0 <= C < HH // 2:
                        pe.wait_ge(hg_cross, C + 1)
                        pe.wait_ge(hg_vt_taken, C + 1)
                        if C > 0:
                            pe.wait_ge(hg_y, C)
                        for i in range(2):
                            v0, v1 = unit(vtok[:, pc, :], 2 * i), unit(vtok[:, pc, :], 2 * i + 1)
                            pe.matmul(SB[3][:, i * T:i * T + P], v0, unit(AA[:, pc, :], 2 * i), start=True, stop=True)
                            pe.matmul(SB[3][:, i * T + P:(i + 1) * T], v0, unit(CR[:, pc, :], i), start=True, stop=False)
                            last = pe.matmul(SB[3][:, i * T + P:(i + 1) * T], v1, unit(AA[:, pc, :], 2 * i + 1), start=False, stop=True)
                        last.then_inc(hg_o, 1)
                    if k == 2 and 0 <= C < HH // 2:
                        pe.wait_ge(hg_sq, C + 1)
                        pe.wait_ge(hg_vt_taken, min(L + 1, HH // 2))
                        pe.matmul(SB[2][:, :], ones, sqo[:, :], start=True, stop=True).then_inc(hg_sum, 1)
                    if it == HH // 2 + 1 and k == 6:
                        p_transposes(1)
            layer_tail(1)

            transposes("att_t", 0, zt, z_ready, [6, 6])
            for c in range(2):
                for q in range(4):
                    pe.wait_ge(x_ready, 16 + q + 1)
                    dense_feature("q_att", c, q, x_hi, x_lo)
            group_start("kv_att", 0)
            bank = pair_of("kv_att", 0)
            for q in range(4):
                wh, wl = unit_ready()
                for kk in range(SPLK):
                    k = q * SPLK + kk
                    for t in range(2):
                        cols = slice(t * P, (t + 1) * P)
                        three(bank[0][:, t * T:(t + 1) * T], (wh[:, kk, cols], wl[:, kk, cols]), (x_hi[:, k, :], x_lo[:, k, :]),
                              start=(k == 0 and t == 0), stop=(k == KT - 1))
                        last = three(bank[1][:, t * P:(t + 1) * P], (x_hi[:, k, cols], x_lo[:, k, cols]),
                                     (wh[:, kk, 2 * P:3 * P], wl[:, kk, 2 * P:3 * P]), start=(k == 0 and t == 0), stop=(k == KT - 1))
                last.then_inc(split_used, 1)
            pe.wait_ge(att_in, 6)
            for t in range(10):
                if t < 8:
                    group_start("score", t)
                    bank = pair_of("score", t)
                    for j in range(2):
                        part = slice(j * AD, (j + 1) * AD)
                        pe.matmul(bank[j][:, 0:T], qa[part, t, P:T], ka[part, t // 4, :], start=True, stop=True)
                        last = pe.matmul(bank[j][:, T:T + P], qa[part, t, 0:P], ka[part, t // 4, 0:P], start=True, stop=True)
                    last.then_inc(turned, 1)
                if 1 <= t < 9:
                    r = t - 1
                    pe.wait_ge(att_prob, r + 1)
                    if r > 0:
                        pe.wait_ge(att_pt0, r)
                    if r > 0:
                        pe.wait_ge(att_pt1, r)
                    for j in range(6):
                        b = SB[2][:, j * P:(j + 1) * P] if j < 4 else SB[3][:, (j - 4) * P:(j - 3) * P]
                        last = pe.transpose(b, lg[:, r % 2, j * P:(j + 1) * P], ident)
                    last.then_inc(att_t, 1)
                if t >= 2:
                    r = t - 2
                    pe.wait_ge(att_pt0, r + 1)
                    pe.wait_ge(att_pt1, r + 1)
                    if r - 1 > 0:
                        pe.wait_ge(att_of, r - 1)
                    v = slice((r // 4) * AD, (r // 4 + 1) * AD)
                    for j in range(2):
                        part = slice(j * AD, (j + 1) * AD)
                        probs = pt[:, r % 2, :]
                        pe.matmul(SB[r % 2][part, 0:P], va[:, 0, v], probs[:, (4 + j) * P:(5 + j) * P], start=True, stop=True)
                        pe.matmul(SB[r % 2][part, P:T], va[:, 0, v], probs[:, 2 * j * P:(2 * j + 1) * P], start=True, stop=False)
                        last = pe.matmul(SB[r % 2][part, P:T], va[:, 1, v], probs[:, (2 * j + 1) * P:(2 * j + 2) * P], start=False, stop=True)
                    last.then_inc(att_o, 1)
            for c in range(2):
                group_start("o_att", c)
                for q in range(4):
                    pe.wait_ge(att_ready, 2 * q + 2)
                    token_unit("o_att", c, q, ya_hi, ya_lo, q == 0, q == 3).then_inc(split_used, 1)

            transposes("mlp_t", 0, zt, z_ready, [8, 8])
            for c in range(8):
                for q in range(4):
                    pe.wait_ge(x_ready, 20 + q + 1)
                    dense_feature("up", c, q, x_hi, x_lo)
            for g in range(4):
                for c in range(2):
                    if g == 0:
                        group_start("down", c)
                    for q in range(4):
                        ch = (8 * g + 2 * q) // 4
                        pe.wait_ge(a_ready, ch + 1)
                        ah, al = act_tiles(ch)
                        wh, wl = unit_ready()
                        bank = pair_of("down", c)
                        for kk in range(SPLK):
                            for t in range(NT):
                                tok = slice(t * P, (t + 1) * P)
                                k = 2 * (q % 2) + kk
                                last = three(bank[t][:, :], (ah[:, k, tok], al[:, k, tok]), (wh[:, kk, :], wl[:, kk, :]),
                                             start=(g == 0 and q == 0 and kk == 0), stop=(g == 3 and q == 3 and kk == 1))
                        last.then_inc(split_used, 1)

        @block.scalar
        def _(act):
            raised = {}
            at = {"unit": 0}

            def link(ins, sem_=act_chain):
                ins.then_inc(sem_, 1)
                settle(sem_)

            def settle(sem_):
                raised[id(sem_)] = raised.get(id(sem_), 0) + 1
                act.wait_ge(sem_, raised[id(sem_)])

            def split_until(end):
                while at["unit"] < min(end, SPLITS):
                    u = at["unit"]
                    act.wait_ge(raw_ready[(u // 2) % NRAW], ready_at[u // 2])
                    if u >= NSPL:
                        act.wait_ge(split_used, u - NSPL + 1)
                        act.wait_ge(lo_done, u - NSPL + 1)
                    act.activation(whi[:, u % NSPL, :], unit_slot(u), ACT.Copy).then_inc(hi_done, 1)
                    at["unit"] += 1

            def group_ready(name, i):
                if (name, i) in UNITS_DONE:
                    act.wait_ge(split_used, UNITS_DONE[(name, i)])
                else:
                    act.wait_ge(turned, TURNED[(name, i)])

            def take_hi(src, hi, base):
                for b in range(4):
                    act.wait_ge(xf_done, base + b + 1)
                    act.activation(hi[:, 2 * b:2 * b + 2, :], src[:, b % 2, :].rearrange("p (k t) -> p k t", k=2), ACT.Copy).then_inc(xhi_done, 1)
                    settle(xhi_done)

            def take_p(layer):
                act.wait_ge(pf_done, layer + 1)
                act.activation(p_hi[:, :, :], pf[:, :, :], ACT.Copy).then_inc(p_hi_done, 1)
                settle(p_hi_done)

            def load_rows(layer):
                act.dma_start(ptk[:, :, :], a["p"][layer, 0].rearrange("(t p) c -> p t c", p=P)).then_inc(p_loaded, 16)
                act.dma_start(gb[:, 0, :], a["ln_g"][layer:layer + 1, :].broadcast_to([P, D])).then_inc(norm_rows, 16)
                act.dma_start(gb[:, 1, :], a["ln_b"][layer:layer + 1, :].broadcast_to([P, D])).then_inc(norm_rows, 16)

            def rstd(eps, scale=1.0):
                act.preload_act_table_set(LOG_TABLES)
                link(act.activation(mv[:, :, 2:3], mv[:, :, 1:2], ACT.Ln, bias=eps, scale=scale))
                act.activation(mv[:, :, 2:3], mv[:, :, 2:3], ACT.Exp, scale=-0.5).then_inc(rstd_done, 1)
                settle(rstd_done)
                act.preload_act_table_set(EXP_TABLES)

            def mean_squares():
                for i in range(NT):
                    act.activation(zt[:, i, :], xtok[:, i, :], ACT.Square, accum_out=mv[:, i, 1:2]).then_inc(squares_done, 1)
                    settle(squares_done)

            for i in range(NT):
                act.dma_start(xtok[:, i, :], a["x"][0, i * P:(i + 1) * P, :]).then_inc(x_loaded, 16)
            act.dma_start(con[:, 0:C_NEG], consts[:, 0:C_NEG]).then_inc(consts_loaded, 16)
            act.dma_start(stA, a["conv_b_w"][0].rearrange("k (t p) -> (k t) p", p=P)).then_inc(stacks_loaded, 16)
            for row, name in ((CONV_A, "conv_a_w"), (LB, "lower_bounds"), (LNG, "ln_g"), (LNB, "ln_b"), (ATTN, "attn_norm_2"),
                              (MLPN, "mlp_norm_2"), (GDNG, "gdn_norm_g"), (HGRNG, "hgrn_norm_g")):
                src = a[name][0] if name == "conv_a_w" else a[name]
                src = src.rearrange("k (t p) -> (k t) p", p=P)
                act.dma_start(GAF[row:row + src.shape[0], 1, 0:P], src).then_inc(stacks_loaded, 16)
            act.dma_start(tail_w[:, :, :], a["w_in_even"][0][:, 8 * D:8 * D + 16].rearrange("(k p) c -> p k c", p=P)).then_inc(tail_loaded, 16)
            act.dma_start(gate_rows[:, 0, :], a["a_log"][0:1, :].broadcast_to([P, GH])).then_inc(rows_loaded, 16)
            act.dma_start(gate_rows[:, 1, :], a["dt_bias"][0:1, :].broadcast_to([P, GH])).then_inc(rows_loaded, 16)
            act.preload_act_table_set(EXP_TABLES)
            split_until(3)
            take_hi(xf0, x_hi, 0)
            split_until(AHEAD)
            act.dma_start(con[:, C_NEG:], consts[:, C_NEG:]).then_inc(consts_loaded, 16)
            act.wait_ge(tail_loaded, 16)
            act.activation(tail_hi[:, :, :], tail_w[:, :, :], ACT.Copy).then_inc(tail_split, 1)
            settle(tail_split)

            def gates():
                act.wait_ge(tail_out, 1)
                act.activation(gt[:, 0:2, :, :].rearrange("p s t h -> p t s h"),
                    SB[1][:, 0:32].rearrange("p (t s h) -> p t s h", t=2, s=2), ACT.Copy).then_inc(tail_copied, 1)
                settle(tail_copied)
                link(act.activation(gt[:, 2, :, :], gt[:, 0, :, :], ACT.Tanh, scale=0.5))
                act.wait_ge(rows_loaded, 32)
                act.activation(gate_rows[:, 0, :], gate_rows[:, 0, :], ACT.Exp).then_inc(gates_tanh, 1)
                settle(gates_tanh)
                act.wait_ge(gates_abs, 1)
                act.preload_act_table_set(LOG_TABLES)
                link(act.activation(gt[:, 4, :, :], gt[:, 4, :, :], ACT.Exp))
                act.activation(gt[:, 4, :, :], gt[:, 4, :, :], ACT.Ln, bias=1.0).then_inc(gates_log, 1)
                settle(gates_log)
                act.preload_act_table_set(EXP_TABLES)

            for h in range(GH):
                split_until(FIRST_SPLIT[("qkvz", h, 0)] + 4 + AHEAD)
                if h == 1:
                    gates()
                group_ready("qkvz", h)
                bank = pair_of("qkvz", h)
                if h > 0:
                    act.wait_ge(conv_done, h)
                act.activation(pad[:, 0:2, 3:T + 3], bank[0][:, :].rearrange("p (s t) -> p s t", s=2), ACT.Copy).then_inc(conv_copied, 1)
                settle(conv_copied)
                act.activation(pad[:, 2, 3:T + 3], bank[1][:, 0:T], ACT.Copy).then_inc(conv_copied, 1)
                settle(conv_copied)
                if h > 0:
                    act.wait_ge(qkv_done, h)
                act.activation(thz[:, :], bank[1][:, T:2 * T], ACT.Tanh, scale=0.5).then_inc(z_tanh, 1)
                settle(z_tanh)
                act.wait_ge(conv_done, h + 1)
                act.activation(th, cv, ACT.Tanh, scale=0.5).then_inc(conv_tanh, 1)
                settle(conv_tanh)
            act.wait_ge(gate_sums, 1)
            act.activation(gt[:, 6, :, :], SB[0][:, 0:2 * GH].rearrange("p (t h) -> p t h", t=2), ACT.Exp).then_inc(gate_exp, 1)
            settle(gate_exp)

            def qk_norm(half):
                act.wait_ge(qkv_done, 4 * half + 4)
                act.wait_ge(gdn_gates, half + 1)
                for n, src in enumerate((qT, qT, kT, kT)):
                    hh = 4 * half + 2 * (n % 2)
                    act.activation((EL if n < 2 else LT)[:, n % 2, :].rearrange("p (h t) -> p h t", h=2), src[:, hh:hh + 2, :],
                        ACT.Square).then_inc(norm_sq, 1)
                    settle(norm_sq)
                act.preload_act_table_set(LOG_TABLES)
                for n in range(4):
                    act.wait_ge(norm_sum, 4 * half + n + 1)
                    dst = (EL if n < 2 else LT)[:, n % 2, :]
                    link(act.activation(dst, SB[n][:, :], ACT.Ln, bias=4e-6))
                    act.activation(dst, dst, ACT.Exp, scale=-0.5).then_inc(norm_rs, 1)
                    settle(norm_rs)
                act.preload_act_table_set(EXP_TABLES)

            def gdn(half, s):
                for g in range(2):
                    A, B = SB[2 * g], SB[2 * g + 1]
                    if s == 0:
                        act.wait_ge(norm_done, 4 * half + 4)
                        act.wait_ge(gdn_products, pe_step(half, 0, g))
                        link(act.activation(EL[:, g, :], A[:, :], ACT.Exp))
                        act.activation(AT[:, g, :], B[:, :], ACT.Exp).then_inc(gdn_exp, 1)
                        settle(gdn_exp)
                    if s == 2 and g == 1:
                        act.wait_ge(gdn_products, pe_step(half, 2, 1))
                        act.activation(QD[:, 0, :], B[:, :], ACT.Exp).then_inc(gdn_exp, 1)
                        settle(gdn_exp)
                    if s == 19:
                        act.wait_ge(gdn_products, pe_step(half, 19, g))
                        act.activation(EL[:, g, :], A[:, :], ACT.Square).then_inc(gdn_squares, 1)
                        settle(gdn_squares)
                    if s == 20:
                        if g == 0:
                            act.preload_act_table_set(LOG_TABLES)
                        act.wait_ge(gdn_products, pe_step(half, 20, g))
                        link(act.activation(KX[:, g, :], B[:, :], ACT.Ln, scale=1.0 / P, bias=EPS))
                        act.activation(KX[:, g, :], KX[:, g, :], ACT.Exp, scale=-0.5).then_inc(gdn_rstd, 1)
                        settle(gdn_rstd)
                if s == 20:
                    act.preload_act_table_set(EXP_TABLES)
                    for g in range(2):
                        act.wait_ge(gdn_gated, 2 * half + g + 1)
                        hh = 4 * half + 2 * g
                        act.activation(yb_hi[:, hh:hh + 2, :], GAF[:, g, :].rearrange("p (h t) -> p h t", h=2), ACT.Copy).then_inc(gdn_hi, 1)
                        settle(gdn_hi)

            def ya(j):
                group_ready("hcbz", j)
                bank = pair_of("hcbz", j)
                if j > 0:
                    act.wait_ge(ya_done, j)
                if GH > 0:
                    act.wait_ge(qkv_done, GH)
                act.activation(hs[:, :], bank[0][:, 0:T], ACT.Copy).then_inc(h_copied, 1)
                settle(h_copied)
                act.activation(thz[:, :], bank[1][:, T:2 * T], ACT.Tanh, scale=0.5).then_inc(h_copied, 1)
                settle(h_copied)
                act.wait_ge(ya_done, j + 1)
                act.activation(ya_hi[:, j, :], yf[:, :], ACT.Copy).then_inc(ya_hi_done, 1)
                settle(ya_hi_done)

            slot = 0
            for half in range(2):
                if half == 0:
                    split_until(FIRST_SPLIT[("hcbz", 0, 0)] + AHEAD)
                qk_norm(half)
                for s in range(GSTEPS):
                    first = FIRST_SPLIT[("hcbz", 0, 0)] + slot if slot < 32 else FIRST_SPLIT[("out_even", 0, 0)] + slot - 32
                    split_until(first + 1 + AHEAD)
                    gdn(half, s)
                    slot += 1
                    if slot <= 32 and slot % 4 == 0:
                        ya(slot // 4 - 1)

            def layer_end(layer):
                load_rows(layer)
                take_p(layer)
                split_until(FIRST_SPLIT[("gate", 2 * layer, 0)] + AHEAD)
                act.wait_ge(mean_done, layer + 1)
                rstd(EPS)
                take_hi(xf, ya_hi, 4 + 8 * layer)
                for c in range(2):
                    split_until(FIRST_SPLIT[("gate", 2 * layer + c, 0)] + 4 + AHEAD)
                    group_ready("gate", 2 * layer + c)
                    bank = pair_of("gate", 2 * layer + c)
                    if 2 * layer + c > 0:
                        act.wait_ge(x2_done, 2 * layer + c)
                    for i in range(NT):
                        act.activation(eg[:, i, :], bank[i][:, :], ACT.Tanh, scale=0.5).then_inc(gate_tanh, 1)
                        settle(gate_tanh)

            act.wait_ge(gdn_ready, 4)
            if KT > 0:
                act.wait_ge(ya_ready, KT)
            layer_end(0)
            take_hi(xf, x_hi, 8)

            act.wait_ge(lb_diff, 1)
            act.activation(lbc[:, 0:2, :], lbc[:, 0:2, :], ACT.Exp).then_inc(lb_exp, 1)
            settle(lb_exp)

            def hg_dense(h):
                p, i = h // 2, h % 2
                group_ready("qfiz", h)
                bank = pair_of("qfiz", h)
                if h - 1 > 0:
                    act.wait_ge(hg_gated, h - 1)
                if p - 1 > 0:
                    act.wait_ge(hg_vt, p - 1)
                link(act.activation(qfth[:, i, :], bank[0][:, :], ACT.Tanh, scale=0.5))
                link(act.activation(zth[:, i, :], bank[1][:, T:2 * T], ACT.Tanh, scale=0.5))
                act.activation(vfm[:, p % 2, i, :], bank[1][:, 0:T], ACT.Copy).then_inc(hg_act, 1)
                settle(hg_act)

            for it in range(HH // 2 + 2):
                C = it - 2
                for k in range(8):
                    if it < HH // 2:
                        split_until(FIRST_SPLIT[("qfiz", 2 * it, 0)] + k + 1 + AHEAD)
                    elif it == HH // 2:
                        split_until(FIRST_SPLIT[("out_odd", 0, 0)] + k + 1 + AHEAD)
                    elif k < 3:
                        split_until(FIRST_SPLIT[("out_odd", 0, 1)] + k + 1 + AHEAD)
                    if k == 0 and 0 < it <= HH // 2:
                        hg_dense(2 * it - 1)
                    if k == 4 and it < HH // 2:
                        hg_dense(2 * it)
                    if 0 <= C < HH // 2:
                        if k == 1:
                            act.wait_ge(hg_o, C + 1)
                            act.activation(sqo[:, :], SB[3][:, :], ACT.Square).then_inc(hg_sq, 1)
                            settle(hg_sq)
                        if k == 2:
                            act.wait_ge(hg_sum, C + 1)
                            if C > 0:
                                act.wait_ge(hg_y, C)
                            act.preload_act_table_set(LOG_TABLES)
                            link(act.activation(rso[:, :], SB[2][:, :], ACT.Ln, scale=1.0 / P, bias=4 * EPS))
                            act.activation(rso[:, :], rso[:, :], ACT.Exp, scale=-0.5).then_inc(hg_rs, 1)
                            settle(hg_rs)
                            act.preload_act_table_set(EXP_TABLES)
                        if k == 3:
                            act.wait_ge(hg_y, C + 1)
                            hi = (ya_hi, yb_hi)[C // 4]
                            act.activation(hi[:, 2 * (C % 4):2 * (C % 4) + 2, :], yo[:, :].rearrange("p (h t) -> p h t", h=2),
                                ACT.Copy).then_inc(hg_hi, 1)
                            settle(hg_hi)
            if HH // 2 > 0:
                act.wait_ge(hg_ready, HH // 2)
            layer_end(1)

            split_until(FIRST_SPLIT[("q_att", 0, 0)] + AHEAD)
            act.wait_ge(x2_done, 4)
            mean_squares()
            rstd(RMS_EPS, 1.0 / D)
            take_hi(xf, x_hi, 16)
            act.dma_start(sink_row[:, :], a["swa_sinks_2"][0:1, :].broadcast_to([P, AH])).then_inc(rows_loaded, 16)
            act.dma_start(gb[:, 0, :], a["final_norm_2"].rearrange("(o n) -> o n", o=1).broadcast_to([P, D])).then_inc(norm_rows, 16)
            for c in range(2):
                split_until(FIRST_SPLIT[("q_att", c, 0)] + 4 + AHEAD)
                group_ready("q_att", c)
                bank = pair_of("q_att", c)
                for b in range(2):
                    act.activation(qa[:, 4 * c + 2 * b:4 * c + 2 * b + 2, :], bank[b][:, :].rearrange("p (k t) -> p k t", k=2),
                        ACT.Copy, scale=AD ** -0.5).then_inc(att_in, 1)
                    settle(att_in)
                act.sem_inc(pair_free[GROUP[("q_att", c)] % 2], 1)
            split_until(FIRST_SPLIT[("o_att", 0, 0)] + AHEAD)
            group_ready("kv_att", 0)
            bank = pair_of("kv_att", 0)
            act.activation(ka[:, :, :], bank[0][:, :].rearrange("p (k t) -> p k t", k=2), ACT.Copy).then_inc(att_in, 1)
            settle(att_in)
            act.activation(va[:, :, :], bank[1][:, 0:2 * P].rearrange("p (k t) -> p k t", k=2), ACT.Copy).then_inc(att_in, 1)
            settle(att_in)
            act.sem_inc(pair_free[GROUP[("kv_att", 0)] % 2], 1)
            for t in range(10):
                if t < 8:
                    act.wait_ge(att_neg, t + 1)
                    for r in range(4):
                        part = lg[:, t % 2, r * T:(r + 1) * T] if r < 2 else lg[:, t % 2, (2 + r) * P:(3 + r) * P]
                        link(act.activation(part, part, ACT.Exp, bias=st_att[:, t % 2, 1, r:r + 1], accum_out=st_att[:, t % 2, 3, r:r + 1]))
                    act.activation(st_att[:, t % 2, 2, :], st_att[:, t % 2, 2, :], ACT.Exp).then_inc(att_exp, 1)
                    settle(att_exp)
                if 1 <= t < 9:
                    if t > 0:
                        act.wait_ge(att_t, t)
                    if t - 2 > 0:
                        act.wait_ge(att_o, t - 2)
                    act.activation(pt[:, (t - 1) % 2, 0:4 * P], SB[2][:, :], ACT.Copy).then_inc(att_pt0, 1)
                    settle(att_pt0)
                if t >= 2:
                    if t - 1 > 0:
                        act.wait_ge(att_of, t - 1)
                    act.activation(ya_hi[:, t - 2, :], ysw[:, t % 2, :], ACT.Copy).then_inc(att_hi, 1)
                    settle(att_hi)
            split_until(FIRST_SPLIT[("up", 0, 0)] + AHEAD)

            act.wait_ge(r_done, 12)
            mean_squares()
            rstd(RMS_EPS, 1.0 / D)
            take_hi(xf, x_hi, 20)
            for c in range(9):
                if c < 8:
                    split_until(FIRST_SPLIT[("up", c, 0)] + 4 + AHEAD)
                    group_ready("up", c)
                    bank = pair_of("up", c)
                    if c - 1 > 0:
                        act.wait_ge(a_ready, c - 1)
                    for b in range(2):
                        act.activation(rl[:, c % 2, 2 * b * T:2 * (b + 1) * T], bank[b][:, :], ACT.Relu).then_inc(relu_done, 1)
                        settle(relu_done)
                    act.sem_inc(pair_free[GROUP[("up", c)] % 2], 1)
                if c >= 1:
                    if c > 0:
                        act.wait_ge(squared, c)
                    act.activation(act_tiles(c - 1)[0], rl[:, (c - 1) % 2, :].rearrange("p (k t) -> p k t", k=4), ACT.Copy).then_inc(a_hi_done, 1)
                    settle(a_hi_done)
            split_until(SPLITS)
            act.wait_ge(r_done, 16)
            mean_squares()
            rstd(RMS_EPS, 1.0 / D)
            for i in range(NT):
                act.wait_ge(final_done, i + 1)
                act.dma_start(out[0, i * P:(i + 1) * P, :], zt[:, i, :]).then_inc(stored, 16)
            act.wait_ge(stored, 16 * NT)

        @block.vector
        def _(vec):
            raised = {}

            def link(ins, sem_=vec_chain):
                ins.then_inc(sem_, 1)
                settle(sem_)

            def settle(sem_):
                raised[id(sem_)] = raised.get(id(sem_), 0) + 1
                vec.wait_ge(sem_, raised[id(sem_)])

            def group_ready(name, i):
                if (name, i) in UNITS_DONE:
                    vec.wait_ge(split_used, UNITS_DONE[(name, i)])
                else:
                    vec.wait_ge(turned, TURNED[(name, i)])

            def free(name, i):
                vec.sem_inc(pair_free[GROUP[(name, i)] % 2], 1)

            def take(name, first, src, hi, lo, base, gain=None, offset=None):
                def low(b):
                    vec.wait_ge(xhi_done, base + b + 1)
                    vec.tensor_tensor(lo[:, 2 * b:2 * b + 2, :], src[:, b % 2, :].rearrange("p (k t) -> p k t", k=2),
                        hi[:, 2 * b:2 * b + 2, :].bitcast(F32), ALU.subtract).then_inc(x_ready, 1)
                    settle(x_ready)

                for b in range(4):
                    c, half = b // 2, b % 2
                    if half == 0:
                        group_ready(name, first + c)
                    bank = pair_of(name, first + c)[half]
                    if gain is None:
                        vec.tensor_copy(src[:, b % 2, :], bank[:, :]).then_inc(xf_done, 1)
                        settle(xf_done)
                    else:
                        for j in range(2):
                            k = 2 * b + j
                            o, i_ = src[:, b % 2, j * T:(j + 1) * T], bank[:, j * T:(j + 1) * T]
                            sig = xf_done if j else vec_chain
                            if offset is None:
                                link(vec.tensor_scalar(o, i_, colB[:, gain + k:gain + k + 1], None, ALU.mult), sig)
                            else:
                                link(vec.tensor_scalar(o, i_, colB[:, gain + k:gain + k + 1], colB[:, offset + k:offset + k + 1],
                                    ALU.mult, ALU.add), sig)
                    if half == 1:
                        free(name, first + c)
                    if b:
                        low(b - 1)
                low(3)

            for z_, w_ in ((pad[:, :, 0:3], 3), (upad[:, 0:2], 2)):
                link(vec.memset(z_, 0.0))
            vec.wait_ge(stack_t, 1)
            link(vec.tensor_copy(colA[:, :], SB[0][:, 0:STACK_A]))
            vec.tensor_copy(colB[:, :], SB[0][:, P:P + STACK_B]).then_inc(cols_taken, 1)
            settle(cols_taken)
            link(vec.tensor_scalar(colB[:, CONV_A:CONV_A + 24], colB[:, CONV_A:CONV_A + 24], 0.5, None, ALU.mult))
            link(vec.tensor_scalar(colB[:, GDNG:HGRNG + 1], colB[:, GDNG:HGRNG + 1], 0.5, None, ALU.mult))
            take("x_t", 0, xf0, x_hi, x_lo, 0)
            vec.wait_ge(tail_split, 1)
            vec.tensor_tensor(tail_lo[:, :, :], tail_w[:, :, :], tail_hi[:, :, :].bitcast(F32), ALU.subtract).then_inc(tail_low, 1)
            settle(tail_low)

            def gates():
                vec.wait_ge(tail_copied, 1)
                vec.wait_ge(rows_loaded, 32)
                link(vec.tensor_tensor(gt[:, 1, :, :], gt[:, 1, :, :], gate_rows[:, 1, :].unsqueeze(1).broadcast_to([P, NT, GH]), ALU.add))
                link(vec.tensor_scalar(gt[:, 4, :, :], gt[:, 1, :, :], -1.0, None, ALU.mult))
                vec.tensor_tensor(gt[:, 4, :, :], gt[:, 4, :, :], gt[:, 1, :, :], ALU.min).then_inc(gates_abs, 1)
                settle(gates_abs)
                vec.wait_ge(gates_tanh, 1)
                link(vec.tensor_scalar(gt[:, 2, :, :], gt[:, 2, :, :], 1.0, 0.5, ALU.add, ALU.mult))
                link(vec.tensor_scalar(gt[:, 3, :, :], gt[:, 2, :, :], 0.5, None, ALU.mult))
                vec.wait_ge(gates_log, 1)
                link(vec.scalar_tensor_tensor(gt[:, 5, :, :], gt[:, 1, :, :], 0.0, gt[:, 4, :, :], ALU.max, ALU.add))
                vec.scalar_tensor_tensor(gt[:, 5, :, :], gt[:, 5, :, :], -1.0,
                    gate_rows[:, 0, :].unsqueeze(1).broadcast_to([P, NT, GH]), ALU.mult, ALU.mult).then_inc(gates_ready, 1)
                settle(gates_ready)

            for h in range(GH):
                if h == 1:
                    gates()
                vec.wait_ge(conv_copied, 2 * h + 2)
                for s in range(3):
                    o = cv[:, s * T:(s + 1) * T]
                    for tap in range(4):
                        w = colA[:, tap * 24 + s * 8 + h:tap * 24 + s * 8 + h + 1]
                        x_ = pad[:, s, tap:tap + T]
                        if tap == 0:
                            link(vec.tensor_scalar(o, x_, w, None, ALU.mult))
                        else:
                            link(vec.scalar_tensor_tensor(o, x_, w, o, ALU.mult, ALU.add), conv_done if (s, tap) == (2, 3) else vec_chain)
                vec.wait_ge(z_tanh, h + 1)
                link(vec.scalar_tensor_tensor(szb[:, h, :], thz[:, :], 1.0, pair_of("qkvz", h)[1][:, T:2 * T], ALU.add, ALU.mult))
                free("qkvz", h)
                vec.wait_ge(conv_tanh, h + 1)
                for s, dst in enumerate((qT, kT, vT)):
                    link(vec.scalar_tensor_tensor(dst[:, h, :], th[:, s * T:(s + 1) * T], 1.0, cv[:, s * T:(s + 1) * T], ALU.add,
                        ALU.mult), qkv_done if s == 2 else vec_chain)
            vec.wait_ge(gate_exp, 1)
            link(vec.tensor_copy(gt[:, 7, 0, :], gt[:, 6, 0, :]))
            link(vec.tensor_tensor(gt[:, 7, 1, :], gt[:, 6, 1, :], gt[:, 2, 1, :], ALU.mult))

            def heads(g, row, half):
                return gt[:, row, g, 4 * half:4 * half + 4].unsqueeze(2).broadcast_to([P, 4, P])

            def four(ap):
                return ap.rearrange("p (u c) -> p u c", u=4)

            def all4(m):
                return m.unsqueeze(1).broadcast_to([P, 4, P])

            def gdn_start(half):
                for g in range(2):
                    link(vec.tensor_tensor(four(GAF[:, g, :]), all4(after), heads(g, 5, half), ALU.mult), gdn_gates if g else vec_chain)
                for n in range(4):
                    vec.wait_ge(norm_rs, 4 * half + n + 1)
                    hh = 4 * half + 2 * (n % 2)
                    dst = (qT if n < 2 else kT)[:, hh:hh + 2, :]
                    rs = (EL if n < 2 else LT)[:, n % 2, :].rearrange("p (h t) -> p h t", h=2)
                    vec.scalar_tensor_tensor(dst, dst, P ** -0.5 if n < 2 else 1.0, rs, ALU.mult, ALU.mult).then_inc(norm_done, 1)
                    settle(norm_done)

            def columns(ap, s, which):
                return ap.rearrange("p (n t r) -> p n t r", t=2, r=s)[:, :, which, :]

            def gdn(half, s):
                for g in range(2):
                    if (s, g) not in DVE_STEPS:
                        continue
                    vec.wait_ge(gdn_products, pe_step(half, s, g))
                    A, B, V = SB[2 * g], SB[2 * g + 1], "gdn_vector"
                    if s == 0:
                        vec.wait_ge(gdn_exp, 3 * half + g + 1)
                        link(vec.tensor_tensor(four(EL[:, g, :]), four(EL[:, g, :]), heads(g, 2, half), ALU.mult))
                        vec.tensor_tensor(four(AT[:, g, :]), four(AT[:, g, :]), all4(upto), ALU.mult).then_inc(gdn_vector, 1)
                        settle(gdn_vector)
                    elif s == 1:
                        link(vec.tensor_tensor(EL[:, g, :], A[:, :], EL[:, g, :], ALU.mult))
                        vec.tensor_tensor(AT[:, g, :], B[:, :], AT[:, g, :], ALU.mult).then_inc(gdn_vector, 1)
                        settle(gdn_vector)
                    elif s == 2:
                        if g == 1:
                            vec.wait_ge(gdn_exp, 3 * half + 3)
                            link(vec.tensor_tensor(four(QD[:, 1, :]), qT[:, 4 * half:4 * half + 4, P:T], four(QD[:, 0, :]), ALU.mult))
                        link(vec.tensor_copy(LT[:, g, :], A[:, :]))
                        link(vec.tensor_tensor(four(XN[:, g, :]), four(EL[:, g, :]), all4(neg[1]), ALU.mult))
                        link(vec.tensor_tensor(four(XN[:, g, :]), four(XN[:, g, :]), all4(ident), ALU.add))
                        link(vec.tensor_tensor(four(XT[:, g, :]), four(LT[:, g, :]), all4(neg1t), ALU.mult))
                        vec.tensor_tensor(four(XT[:, g, :]), four(XT[:, g, :]), all4(ident), ALU.add).then_inc(gdn_vector, 1)
                        settle(gdn_vector)
                    elif s == 3:
                        link(vec.tensor_tensor(four(KX[:, g, :]), four(A[:, :]), heads(g, 7, half), ALU.mult))
                        vec.tensor_tensor(four(VB[:, g, :]), four(B[:, :]), heads(g, 3, half), ALU.mult).then_inc(gdn_vector, 1)
                        settle(gdn_vector)
                    elif s < 16:
                        lv = LEVELS[(s - 4) // 2 + 1]
                        if s % 2 == 0:
                            vec.tensor_tensor(four(EL[:, g, :]), four(A[:, :]), all4(neg[lv]), ALU.mult).then_inc(gdn_vector, 1)
                            settle(gdn_vector)
                        else:
                            if s != 15:
                                o = columns(XN[:, g, :], lv, 0)
                                link(vec.tensor_tensor(o, B[:, 0:256].rearrange("p (n r) -> p n r", r=lv), o, ALU.add))
                            o = columns(XT[:, g, :], lv, 1)
                            vec.tensor_tensor(o, B[:, 256:512].rearrange("p (n r) -> p n r", r=lv), o, ALU.add).then_inc(gdn_vector, 1)
                            settle(gdn_vector)
                    elif s == 16 and g == 0:
                        vec.tensor_copy(XN[:, 0, :], A[:, :]).then_inc(gdn_vector, 1)
                        settle(gdn_vector)
                    elif s == 16:
                        vec.tensor_scalar(LT[:, 1, :], A[:, :], -1.0, None, ALU.mult).then_inc(gdn_vector, 1)
                        settle(gdn_vector)
                    elif s == 17:
                        vec.tensor_copy(LT[:, 0, :], B[:, :]).then_inc(gdn_vector, 1)
                        settle(gdn_vector)
                    elif s == 18:
                        vec.tensor_copy(XN[:, 1, :], A[:, :]).then_inc(gdn_vector, 1)
                        settle(gdn_vector)
                    elif s == 20:
                        vec.wait_ge(gdn_rstd, 2 * half + g + 1)
                        hh = 4 * half + 2 * g
                        vec.tensor_tensor(GAF[:, g, :], A[:, :], KX[:, g, :], ALU.mult).then_inc(gdn_vector, 1)
                        settle(gdn_vector)
                        y = GAF[:, g, :].rearrange("p (h t) -> p h t", h=2)
                        vec.scalar_tensor_tensor(y, y, colB[:, GDNG:GDNG + 1], szb[:, hh:hh + 2, :], ALU.mult, ALU.mult).then_inc(gdn_gated, 1)
                        settle(gdn_gated)
                if s == 20:
                    for g in range(2):
                        vec.wait_ge(gdn_hi, 2 * half + g + 1)
                        hh = 4 * half + 2 * g
                        vec.tensor_tensor(yb_lo[:, hh:hh + 2, :], GAF[:, g, :].rearrange("p (h t) -> p h t", h=2),
                            yb_hi[:, hh:hh + 2, :].bitcast(F32), ALU.subtract).then_inc(gdn_ready, 1)
                        settle(gdn_ready)

            def ya(j):
                vec.wait_ge(h_copied, 2 * j + 2)
                bank = pair_of("hcbz", j)
                link(vec.tensor_tensor(upad[:, 2:T + 2], bank[0][:, T:2 * T], hs[:, :], ALU.mult))
                for tap in range(3):
                    w = colB[:, CONV_A + tap * 8 + j:CONV_A + tap * 8 + j + 1]
                    if tap == 0:
                        link(vec.tensor_scalar(yf[:, :], upad[:, 0:T], w, None, ALU.mult))
                    else:
                        link(vec.scalar_tensor_tensor(yf[:, :], upad[:, tap:tap + T], w, yf[:, :], ALU.mult, ALU.add))
                link(vec.tensor_tensor(yf[:, :], bank[1][:, 0:T], yf[:, :], ALU.mult))
                link(vec.scalar_tensor_tensor(hs[:, :], thz[:, :], 1.0, bank[1][:, T:2 * T], ALU.add, ALU.mult))
                free("hcbz", j)
                vec.tensor_tensor(yf[:, :], yf[:, :], hs[:, :], ALU.mult).then_inc(ya_done, 1)
                settle(ya_done)

            def ya_low(j):
                vec.wait_ge(ya_hi_done, j + 1)
                vec.tensor_tensor(ya_lo[:, j, :], yf[:, :], ya_hi[:, j, :].bitcast(F32), ALU.subtract).then_inc(ya_ready, 1)
                settle(ya_ready)

            vec.wait_ge(consts_loaded, 32)
            slot = 0
            for half in range(2):
                gdn_start(half)
                for s in range(GSTEPS):
                    gdn(half, s)
                    slot += 1
                    if slot <= 32 and slot % 4 == 0:
                        ya(slot // 4 - 1)
                    if slot <= 33 and slot % 4 == 1 and slot > 4:
                        ya_low(slot // 4 - 1)

            def take_p(layer):
                vec.wait_ge(p_t, layer + 1)
                vec.tensor_copy(pf[:, :, :], SB[0][:, :].rearrange("p (k t) -> p k t", k=2)).then_inc(pf_done, 1)
                settle(pf_done)
                vec.wait_ge(p_hi_done, layer + 1)
                vec.tensor_tensor(p_lo[:, :, :], pf[:, :, :], p_hi[:, :, :].bitcast(F32), ALU.subtract).then_inc(p_ready, 1)
                settle(p_ready)

            def residual(name, first, alpha):
                for c in range(2):
                    group_ready(name, first + c)
                    bank = pair_of(name, first + c)
                    for i in range(NT):
                        o = xtok[:, i, c * COLS:(c + 1) * COLS]
                        vec.scalar_tensor_tensor(o, o, alpha, bank[i][:, :], ALU.mult, ALU.add).then_inc(r_done, 1)
                        settle(r_done)
                    free(name, first + c)

            def layer_end(layer):
                take_p(layer)
                residual(("out_even", "out_odd")[layer], 0, ALPHA)
                for i in range(NT):
                    for c in range(2):
                        link(vec.bn_stats(stats[:, i, c, :], xtok[:, i, c * COLS:(c + 1) * COLS]))
                    link(vec.bn_aggr(mv[:, i, 0:2], stats[:, i, :, :].rearrange("p c s -> p (c s)")), mean_done if i else vec_chain)
                vec.wait_ge(rstd_done, layer + 1)
                for i in range(NT):
                    vec.tensor_scalar(zt[:, i, :], xtok[:, i, :], mv[:, i, 0:1], mv[:, i, 2:3], ALU.subtract, ALU.mult).then_inc(z_ready, 1)
                    settle(z_ready)
                take("ln_t", 2 * layer, xf, ya_hi, ya_lo, 4 + 8 * layer, LNG + 8 * layer, LNB + 8 * layer)
                if 32 * (layer + 1) > 0:
                    vec.wait_ge(norm_rows, 32 * (layer + 1))
                for i in range(NT):
                    link(vec.tensor_tensor(xtok[:, i, :], zt[:, i, :], gb[:, 0, :], ALU.mult))
                    link(vec.tensor_tensor(xtok[:, i, :], xtok[:, i, :], gb[:, 1, :], ALU.add))
                vec.wait_ge(split_used, FIRST_SPLIT[("pl", layer, 0)] + 2)
                for c in range(2):
                    for i in range(NT):
                        vec.wait_ge(gate_tanh, 4 * layer + 2 * c + i + 1)
                        link(vec.scalar_tensor_tensor(eg[:, i, :], eg[:, i, :], 1.0, SB[2 * i + c][:, :], ALU.add, ALU.mult))
                        o = xtok[:, i, c * COLS:(c + 1) * COLS]
                        link(vec.scalar_tensor_tensor(o, eg[:, i, :], 0.5, o, ALU.mult, ALU.add), x2_done if i else vec_chain)
                    free("gate", 2 * layer + c)

            layer_end(0)
            take("x2_t", 0, xf, x_hi, x_lo, 8)

            for i in range(2):
                link(vec.memset(AA[:, i, :], 0.0))
            l0, l1 = colB[:, LB:LB + HH], colB[:, LB + HH:LB + 2 * HH]
            link(vec.tensor_tensor(lbc[:, 2, :], l0, l1, ALU.max))
            link(vec.tensor_tensor(lbc[:, 0, :], l0, lbc[:, 2, :], ALU.subtract))
            vec.tensor_tensor(lbc[:, 1, :], l1, lbc[:, 2, :], ALU.subtract).then_inc(lb_diff, 1)
            settle(lb_diff)
            vec.wait_ge(lb_exp, 1)
            link(vec.tensor_tensor(lbc[:, 2, :], lbc[:, 0, :], lbc[:, 1, :], ALU.add))
            link(vec.reciprocal(lbc[:, 3, :], lbc[:, 2, :]))
            link(vec.tensor_tensor(lbc[:, 3, :], lbc[:, 3, :], lbc[:, 1, :], ALU.mult))
            link(vec.tensor_scalar(lbc[:, 4, :], lbc[:, 3, :], 0.5, 0.5, ALU.mult, ALU.add))
            vec.tensor_scalar(lbc[:, 5, :], lbc[:, 3, :], -0.5, 0.5, ALU.mult, ALU.add).then_inc(lb_done, 1)
            settle(lb_done)

            def hg_gate(h):
                p, i = h // 2, h % 2
                par, cols = p % 2, slice(i * T, (i + 1) * T)
                vec.wait_ge(hg_act, h + 1)
                if p - 1 > 0:
                    vec.wait_ge(hg_cross_mm, p - 1)
                bank = pair_of("qfiz", h)
                link(vec.scalar_tensor_tensor(q0[:, par, cols], qfth[:, i, 0:T], 1.0, bank[0][:, 0:T], ALU.add, ALU.mult))
                link(vec.scalar_tensor_tensor(szo[:, p % 3, cols], zth[:, i, :], 1.0, bank[1][:, T:2 * T], ALU.add, ALU.mult))
                free("qfiz", h)
                link(vec.tensor_scalar(F0[:, par, cols], qfth[:, i, T:2 * T], lbc[:, 5, h:h + 1], lbc[:, 4, h:h + 1], ALU.mult, ALU.add))
                link(vec.tensor_scalar(KS[:, par, cols], F0[:, par, cols], -1.0, 1.0, ALU.mult, ALU.add))
                vec.tensor_tensor(QS[:, par, cols], q0[:, par, cols], F0[:, par, cols], ALU.mult).then_inc(hg_gated, 1)
                settle(hg_gated)

            f_at = {1: 0}
            for n, s in enumerate(LEVELS[1:]):
                f_at[s] = sum(2 * T // x for x in LEVELS[1:1 + n])

            def decay(par, s, which):
                blocks = F0[:, par, :] if s == 1 else F1[:, f_at[s]:f_at[s] + 2 * T // s]
                return blocks.rearrange("p (n t) -> p n t", t=2)[:, :, which:which + 1]

            def level(par, L, k):
                s = LEVELS[k - 1]
                vec.wait_ge(hg_level_mm, 7 * L + k)
                n_ = 64 // s
                if k == 1:
                    link(vec.copy_predicated(four(AA[:, par, :]), all4(ident).bitcast(I32), four(SB[0][:, :])))
                o = AA[:, par, :].rearrange("p (u m t r) -> p u m t r", u=4, t=2, r=s)[:, :, :, 1, :]
                m = pick[s].rearrange("p (m r) -> p m r", r=s).unsqueeze(1).broadcast_to([P, 4, n_, s])
                link(vec.copy_predicated(o, m, SB[k % 2][:, 0:256].rearrange("p (u m r) -> p u m r", u=4, r=s)))
                n2 = 2 * T // (2 * s)
                if s < 64:
                    link(vec.tensor_tensor(F1[:, f_at[2 * s]:f_at[2 * s] + n2].unsqueeze(2), decay(par, s, 0), decay(par, s, 1), ALU.mult))
                o = columns(QS[:, par, :], s, 1)
                link(vec.tensor_tensor(o, o, decay(par, s, 0).broadcast_to([P, n2, s]), ALU.mult))
                o = columns(KS[:, par, :], s, 0)
                vec.tensor_tensor(o, o, decay(par, s, 1).broadcast_to([P, n2, s]), ALU.mult).then_inc(hg_level, 1)
                settle(hg_level)

            for it in range(HH // 2 + 2):
                L, C = it - 1, it - 2
                for k in range(8):
                    if k == 0 and 0 <= L < HH // 2:
                        hg_gate(2 * L + 1)
                        vec.wait_ge(hg_vt, L + 1)
                        if L - 1 > 0:
                            vec.wait_ge(hg_o, L - 1)
                        vec.tensor_copy(vtok[:, L % 2, :], SB[2][:, :]).then_inc(hg_vt_taken, 1)
                        settle(hg_vt_taken)
                    if k == 0 and 0 <= C < HH // 2:
                        vec.wait_ge(hg_cross_mm, C + 1)
                        vec.tensor_copy(CR[:, C % 2, :], SB[0][:, 0:2 * P]).then_inc(hg_cross, 1)
                        settle(hg_cross)
                    if k >= 1 and 0 <= L < HH // 2:
                        level(L % 2, L, k)
                    if k == 4 and it < HH // 2:
                        hg_gate(2 * it)
                    if k == 3 and 0 <= C < HH // 2:
                        vec.wait_ge(hg_rs, C + 1)
                        link(vec.tensor_tensor(yo[:, :], SB[3][:, :], rso[:, :], ALU.mult))
                        vec.scalar_tensor_tensor(yo[:, :], yo[:, :], colB[:, HGRNG:HGRNG + 1], szo[:, C % 3, :], ALU.mult, ALU.mult).then_inc(hg_y, 1)
                        settle(hg_y)
                    if k == 4 and 0 <= C < HH // 2:
                        vec.wait_ge(hg_hi, C + 1)
                        hi, lo = ((ya_hi, ya_lo), (yb_hi, yb_lo))[C // 4]
                        tiles = slice(2 * (C % 4), 2 * (C % 4) + 2)
                        vec.tensor_tensor(lo[:, tiles, :], yo[:, :].rearrange("p (h t) -> p h t", h=2), hi[:, tiles, :].bitcast(F32),
                            ALU.subtract).then_inc(hg_ready, 1)
                        settle(hg_ready)
            layer_end(1)

            def rms(n, base, gain):
                if n > 0:
                    vec.wait_ge(rstd_done, n)
                for i in range(NT):
                    vec.tensor_scalar(zt[:, i, :], xtok[:, i, :], mv[:, i, 2:3], None, ALU.mult).then_inc(z_ready, 1)
                    settle(z_ready)

            rms(3, 16, ATTN)
            take("att_t", 0, xf, x_hi, x_lo, 16, ATTN)
            for h in range(AH):
                link(vec.tensor_scalar(bias[:, h, :], ndist, 2.0 ** (-8.0 * (h + 1) / AH), None, ALU.mult), bias_done if h == AH - 1 else vec_chain)
            vec.wait_ge(rows_loaded, 48)

            def scores(t):
                group_ready("score", t)
                bank = pair_of("score", t)
                par = t % 2
                if t - 1 > 0:
                    vec.wait_ge(att_t, t - 1)
                for j in range(2):
                    link(vec.tensor_tensor(lg[:, par, j * T:(j + 1) * T], bank[j][:, 0:T], bias[:, 2 * t + j, :], ALU.add))
                    link(vec.tensor_tensor(lg[:, par, (4 + j) * P:(5 + j) * P], bank[j][:, T:T + P], bias[:, 2 * t + j, P:2 * P], ALU.add))
                free("score", t)
                link(vec.tensor_reduce(st_att[:, par, 0, 0:2], lg[:, par, 0:4 * P].rearrange("p (h c) -> p h c", h=2), AX_X, ALU.max))
                link(vec.tensor_reduce(st_att[:, par, 0, 2:4], lg[:, par, 4 * P:6 * P].rearrange("p (h c) -> p h c", h=2), AX_X, ALU.max))
                sink = sink_row[:, 2 * t:2 * t + 2].unsqueeze(1).broadcast_to([P, 2, 2])
                mx = st_att[:, par, 0, :].rearrange("p (b h) -> p b h", b=2)
                link(vec.tensor_tensor(mx, mx, sink, ALU.max))
                link(vec.tensor_tensor(st_att[:, par, 2, :].rearrange("p (b h) -> p b h", b=2), sink, mx, ALU.subtract))
                vec.tensor_scalar(st_att[:, par, 1, :], st_att[:, par, 0, :], -1.0, None, ALU.mult).then_inc(att_neg, 1)
                settle(att_neg)

            def probs(t):
                par = t % 2
                vec.wait_ge(att_exp, t + 1)
                link(vec.tensor_tensor(st_att[:, par, 3, :], st_att[:, par, 3, :], st_att[:, par, 2, :], ALU.add))
                link(vec.reciprocal(st_att[:, par, 3, :], st_att[:, par, 3, :]))
                for r in range(4):
                    part = lg[:, par, r * T:(r + 1) * T] if r < 2 else lg[:, par, (2 + r) * P:(3 + r) * P]
                    link(vec.tensor_scalar(part, part, st_att[:, par, 3, r:r + 1], None, ALU.mult), att_prob if r == 3 else vec_chain)

            for t in range(11):
                if t < 8:
                    scores(t)
                if 1 <= t < 9:
                    probs(t - 1)
                    if t > 0:
                        vec.wait_ge(att_t, t)
                    if t - 2 > 0:
                        vec.wait_ge(att_o, t - 2)
                    vec.tensor_copy(pt[:, (t - 1) % 2, 4 * P:6 * P], SB[3][:, 0:2 * P]).then_inc(att_pt1, 1)
                    settle(att_pt1)
                if 2 <= t < 10:
                    if t - 1 > 0:
                        vec.wait_ge(att_o, t - 1)
                    if t - 3 > 0:
                        vec.wait_ge(att_hi, t - 3)
                    vec.tensor_copy(ysw[:, t % 2, :], SB[t % 2][:, 0:T]).then_inc(att_of, 1)
                    settle(att_of)
                if t >= 3:
                    r = t - 3
                    vec.wait_ge(att_hi, r + 1)
                    vec.tensor_tensor(ya_lo[:, r, :], ysw[:, r % 2, :], ya_hi[:, r, :].bitcast(F32), ALU.subtract).then_inc(att_ready, 1)
                    settle(att_ready)
            residual("o_att", 0, 1.0)
            rms(4, 20, MLPN)
            take("mlp_t", 0, xf, x_hi, x_lo, 20, MLPN)
            for c in range(9):
                if c < 8:
                    vec.wait_ge(relu_done, 2 * c + 2)
                    vec.tensor_tensor(rl[:, c % 2, :], rl[:, c % 2, :], rl[:, c % 2, :], ALU.mult).then_inc(squared, 1)
                    settle(squared)
                if c >= 1:
                    if c > 0:
                        vec.wait_ge(a_hi_done, c)
                    hi, lo = act_tiles(c - 1)
                    vec.tensor_tensor(lo, rl[:, (c - 1) % 2, :].rearrange("p (k t) -> p k t", k=4), hi.bitcast(F32),
                        ALU.subtract).then_inc(a_ready, 1)
                    settle(a_ready)
            residual("down", 0, 1.0)
            vec.wait_ge(rstd_done, 5)
            vec.wait_ge(norm_rows, 80)
            for i in range(NT):
                link(vec.tensor_scalar(zt[:, i, :], xtok[:, i, :], mv[:, i, 2:3], None, ALU.mult))
                vec.tensor_tensor(zt[:, i, :], zt[:, i, :], gb[:, 0, :], ALU.mult).then_inc(final_done, 1)
                settle(final_done)


def shape_constants():
    import numpy as np

    i, j = np.arange(P)[:, None], np.arange(P)[None, :]
    out = np.zeros((P, C_ALL), np.float32)
    out[:, C_ID:C_ID + P] = i == j
    out[:, C_UPTO:C_UPTO + P] = i <= j
    out[:, C_AFTER:C_AFTER + P] = i > j
    out[:, C_ONES:C_ONES + P] = 1
    for n, s in enumerate(LEVELS):
        below = (i // s % 2 == 1) & (j // s == i // s - 1)
        out[:, C_NEG + n * P:C_NEG + (n + 1) * P] = np.where(below, -1, 0)
        out[:, C_PICK + n * 64:C_PICK + (n + 1) * 64] = below.T.reshape(P, P // (2 * s), 2, s)[:, :, 1, :].reshape(P, 64)
        if s == 1:
            out[:, C_NEG1T:C_NEG1T + P] = np.where(below.T, -1, 0)
    key = np.arange(2 * P)[None, :]
    dist = P + i - key
    out[:, C_DIST:C_DIST + 2 * P] = np.where((dist >= 0) & (dist < P), -dist, -1e30)
    return out


_INS = ["x", "p", "w_in_even", "conv_a_w", "conv_b_w", "a_log", "dt_bias", "gdn_norm_g", "w_out_even", "w_in_odd",
        "lower_bounds", "hgrn_norm_g", "w_out_odd", "ln_g", "ln_b", "w_pl", "w_pl_gate", "attn_norm_2", "mlp_norm_2",
        "final_norm_2", "swa_w_qkv_2", "swa_sinks_2", "swa_w_o_2", "mlp_w_up_2", "mlp_w_down_2"]


def kernel(**inputs):
    import numpy as _np
    import concourse.bacc as _bacc
    from concourse import mybir as _mybir
    from concourse.bass_utils import run_bass_kernel_spmd as _run

    nc = _bacc.Bacc("TRN2", target_bir_lowering=False, num_devices=1)
    arrays, args = {}, {}
    for name in _INS:
        x = _np.ascontiguousarray(inputs[name])
        arrays[f"in_{name}_dram"] = x
        args[name] = nc.dram_tensor(f"in_{name}_dram", x.shape, _mybir.dt.from_np(x.dtype), kind="ExternalInput").ap()
    table = shape_constants()
    arrays["shape_constants_dram"] = table
    consts = nc.dram_tensor("shape_constants_dram", table.shape, F32, kind="ExternalInput").ap()
    out = nc.dram_tensor("out_0_dram", (1, T, D), F32, kind="ExternalOutput").ap()
    build(nc, args, consts, out)
    r = _run(nc, [arrays], core_ids=[0])
    return r.results[0]["out_0_dram"]
```

```python
from contextlib import ExitStack

import concourse.bass as bass
from concourse import mybir

F32 = mybir.dt.float32
F32R = mybir.dt.float32r
I32 = mybir.dt.int32
ALU = mybir.AluOpType
ACT = mybir.ActivationFunctionType
AX_X = mybir.AxisListType.X

P = 128
T = 256
NT = T // P
D = 1024
KT = D // P
COLS = 512
RAWK = 4
SPLK = 2
NRAW = 3
NSPL = 6
AHEAD = 5
GH = 8
HH = 16
AH = 16
AD = 64
ALPHA = 4.0 ** 0.25
EPS = 1e-5
RMS_EPS = 1e-6
LEVELS = [1, 2, 4, 8, 16, 32, 64]
STACK_A = 96
CONV_A, LB, LNG, LNB, ATTN, MLPN, GDNG, HGRNG, STACK_B = 0, 24, 56, 72, 88, 96, 104, 105, 106

C_ID, C_UPTO, C_AFTER, C_ONES = 0, P, 2 * P, 3 * P
C_NEG = 4 * P
C_NEG1T = C_NEG + len(LEVELS) * P
C_PICK = C_NEG1T + P
C_DIST = C_PICK + len(LEVELS) * P // 2
C_ALL = C_DIST + 3 * P
EXP_TABLES = "exp_and_others"
LOG_TABLES = "natural_log_exp_and_others"


class Count:

    def __init__(self, sem):
        self.sem = sem
        self.n = 0


def load_list():
    def chunks(name, first, n):
        return [(name, first + i, 0, half) for i in range(n) for half in range(2)]

    def out_projection(name):
        first = [(name, c, 0, half) for c in range(2) for half in range(2)]
        return first + [(name, c, 1, half) for half in range(2) for c in range(2)]

    out = chunks("qkvz", 0, GH) + chunks("hcbz", 0, KT) + out_projection("out_even")
    out += [("pl", 0, 0, 0)] + chunks("gate", 0, 2)
    out += chunks("qfiz", 0, HH) + out_projection("out_odd")
    out += [("pl", 1, 0, 0)] + chunks("gate", 2, 2)
    out += chunks("q_att", 0, 1) + chunks("kv_att", 0, 1) + chunks("q_att", 1, 1)
    out += [("o_att", c, 0, half) for half in range(2) for c in range(2)]
    out += chunks("up", 0, 8) + [("down", c, g, half) for g in range(4) for c in range(2) for half in range(2)]
    return out


LOADS = load_list()
SPLITS = 2 * len(LOADS)
FIRST_SPLIT = {}
UNITS_DONE = {}
for _n, (_name, _i, _g, _half) in enumerate(LOADS):
    FIRST_SPLIT.setdefault((_name, _i, _g), 2 * _n)
    if _name != "pl":
        UNITS_DONE[(_name, _i)] = 2 * _n + 2
GROUPS = [("x_t", 0), ("x_t", 1)] + [("qkvz", h) for h in range(GH)] + [("hcbz", j) for j in range(KT)]
GROUPS += [("out_even", 0), ("out_even", 1), ("ln_t", 0), ("ln_t", 1), ("gate", 0), ("gate", 1), ("x2_t", 0), ("x2_t", 1)]
GROUPS += [("qfiz", h) for h in range(HH)]
GROUPS += [("out_odd", 0), ("out_odd", 1), ("ln_t", 2), ("ln_t", 3), ("gate", 2), ("gate", 3), ("att_t", 0), ("att_t", 1)]
GROUPS += [("q_att", 0), ("kv_att", 0), ("q_att", 1)] + [("score", t) for t in range(8)]
GROUPS += [("o_att", 0), ("o_att", 1), ("mlp_t", 0), ("mlp_t", 1)] + [("up", c) for c in range(8)] + [("down", 0), ("down", 1)]
PAIR, BEFORE = {}, {}
_used, _last = [0, 0], 1
for _g in GROUPS:
    PAIR[_g] = _last if _g[0] == "score" and _g[1] > 0 else 1 - _last
    BEFORE[_g] = _used[PAIR[_g]]
    _used[PAIR[_g]] += 1
    _last = PAIR[_g]
TURNED = {g: i + 1 for i, g in enumerate(g for g in GROUPS if g not in UNITS_DONE)}

GSTEPS = 21
LEAD = 4
BESIDE = 44
PE_STEPS = [(s, g) for s in range(GSTEPS) for g in range(2) if (s, g) not in ((17, 1), (18, 0))]
DVE_STEPS = [(s, g) for s, g in PE_STEPS if s != 19]


def pe_step(half, s, g):
    return half * len(PE_STEPS) + PE_STEPS.index((s, g)) + 1


def dve_step(half, s, g):
    return half * len(DVE_STEPS) + DVE_STEPS.index((s, g)) + 1


def build(nc, a, consts, out):
    with ExitStack() as ctx:
        def sem(name):
            return ctx.enter_context(nc.semaphore(name))

        def sb(name, shape, dt=F32, stack=ctx):
            return stack.enter_context(nc.sbuf_tensor(name, shape, dt))

        raw = sb("raw", [P, NRAW, RAWK * COLS])
        whi = sb("whi", [P, NSPL, SPLK * COLS], F32R)
        wlo = sb("wlo", [P, NSPL, SPLK * COLS], F32R)
        con = sb("con", [P, C_ALL])
        colA = sb("colA", [P, STACK_A])
        colB = sb("colB", [P, STACK_B])
        xtok = sb("xtok", [P, NT, D])
        x_hi = sb("x_hi", [P, KT, T], F32R)
        x_lo = sb("x_lo", [P, KT, T], F32R)
        ya_hi = sb("ya_hi", [P, KT, T], F32R)
        ya_lo = sb("ya_lo", [P, KT, T], F32R)
        with ExitStack() as ph:
            qT = sb("qT", [P, GH, T], stack=ph)
            kT = sb("kT", [P, GH, T], stack=ph)
        with ExitStack() as ph:
            lg = sb("lg", [P, 3, 6 * P], stack=ph)
            pt = sb("pt", [P, 2, 6 * P], stack=ph)
        yb_hi = sb("yb_hi", [P, GH, T], F32R)
        yb_lo = sb("yb_lo", [P, GH, T], F32R)

        ident = con[:, C_ID:C_ID + P]
        upto = con[:, C_UPTO:C_UPTO + P]
        after = con[:, C_AFTER:C_AFTER + P]
        ones = con[:, C_ONES:C_ONES + P]
        neg = {s: con[:, C_NEG + i * P:C_NEG + (i + 1) * P] for i, s in enumerate(LEVELS)}
        neg1t = con[:, C_NEG1T:C_NEG1T + P]
        pick = {s: con[:, C_PICK + 64 * i:C_PICK + 64 * (i + 1)].bitcast(I32) for i, s in enumerate(LEVELS)}
        ndist = con[:, C_DIST:C_DIST + 3 * P]

        with ExitStack() as ph:
            vT = sb("vT", [P, GH, T], stack=ph)
            szb = sb("szb", [P, GH, T], stack=ph)
            pad = sb("pad", [P, 3, T + 4], stack=ph)
            thz = sb("thz", [P, T], stack=ph)
            hs = sb("hs", [P, T], stack=ph)
            upad = sb("upad", [P, T + 2], stack=ph)
            yf = sb("yf", [P, T], stack=ph)
            tail_w = sb("tail_w", [P, KT, 16], stack=ph)
            tail_hi = sb("tail_hi", [P, KT, 16], F32R, stack=ph)
            tail_lo = sb("tail_lo", [P, KT, 16], F32R, stack=ph)
            gate_rows = sb("gate_rows", [P, 2, GH], stack=ph)
            gt = sb("gt", [P, 8, NT, GH], stack=ph)
            GAF = sb("GAF", [P, 2, 4 * P], stack=ph)
            EL = sb("EL", [P, 2, 4 * P], stack=ph)
            AT = sb("AT", [P, 2, 4 * P], stack=ph)
            LT = sb("LT", [P, 2, 4 * P], stack=ph)
            XN = sb("XN", [P, 2, 4 * P], stack=ph)
            XT = sb("XT", [P, 2, 4 * P], stack=ph)
            KX = sb("KX", [P, 2, 4 * P], stack=ph)
            VB = sb("VB", [P, 2, 4 * P], stack=ph)
            QD = sb("QD", [P, 2, 4 * P], stack=ph)
            cv = AT[:, :, :].rearrange("p g c -> p (g c)")[:, 0:3 * T]
            th = KX[:, :, :].rearrange("p g c -> p (g c)")[:, 0:3 * T]
            xf0 = VB
            stA = GAF[0:STACK_A, 0, 0:P]
            stB = GAF[0:STACK_B, 1, 0:P]
        with ExitStack() as ph:
            qfth = sb("qfth", [P, 2, 2 * T], stack=ph)
            zth = sb("zth", [P, 2, T], stack=ph)
            vfm = sb("vfm", [P, 2, 2, T], stack=ph)
            q0 = sb("q0", [P, 2, 2 * T], stack=ph)
            QS = sb("QS", [P, 2, 2 * T], stack=ph)
            KS = sb("KS", [P, 2, 2 * T], stack=ph)
            F0 = sb("F0", [P, 2, 2 * T], stack=ph)
            F1 = sb("F1", [P, 2 * T], stack=ph)
            AA = sb("AA", [P, 2, 4 * P], stack=ph)
            CR = sb("CR", [P, 2, 2 * P], stack=ph)
            vtok = sb("vtok", [P, 2, 4 * P], stack=ph)
            szo = sb("szo", [P, 3, 2 * T], stack=ph)
            sqo = sb("sqo", [P, 2 * T], stack=ph)
            rso = sb("rso", [P, 2 * T], stack=ph)
            yo = sb("yo", [P, 2 * T], stack=ph)
            lbc = sb("lbc", [P, 6, HH], stack=ph)
        zt = sb("zt", [P, NT, D])
        gb = sb("gb", [P, 2, D])
        eg = sb("eg", [P, 2, COLS])
        xf = sb("xf", [P, 2, 2 * T])
        ptk = sb("ptk", [P, NT, T])
        pf = sb("pf", [P, NT, T])
        p_hi = sb("p_hi", [P, NT, T], F32R)
        p_lo = sb("p_lo", [P, NT, T], F32R)
        stats = sb("stats", [P, NT, 2, 6])
        mv = sb("mv", [P, NT, 4])
        root = sb("root", [P, T])
        rl = zt
        with ExitStack() as ph:
            qa = sb("qa", [P, KT, T], stack=ph)
            ka = sb("ka", [P, 2, T], stack=ph)
            va = sb("va", [P, 2, P], stack=ph)
            dg = sb("dg", [P, 2, 4 * P], stack=ph)
            rsum = sb("rsum", [P, 2, 4], stack=ph)
            sink_row = sb("sink_row", [P, AH], stack=ph)
            nsink = sb("nsink", [P, AH], stack=ph)
            st_att = sb("st_att", [P, 2, 4, 4], stack=ph)
        ac_hi = sb("ac_hi", [P, 16, T], F32R)
        ac_lo = sb("ac_lo", [P, 16, T], F32R)

        def act_tiles(c):
            hi, lo, b = ((ya_hi, ya_lo, 0), (yb_hi, yb_lo, 8))[c // 2] if c < 4 else (ac_hi, ac_lo, 16)
            return hi[:, 4 * c - b:4 * c - b + 4, :], lo[:, 4 * c - b:4 * c - b + 4, :]

        DB = [[ctx.enter_context(nc.psum_tensor(f"dense{i}{j}", [P, 512], F32)) for j in range(2)] for i in range(2)]
        SB = [ctx.enter_context(nc.psum_tensor(f"bank{i}", [P, 512], F32)) for i in range(4)]

        raw_ready = [sem(f"raw_ready{i}") for i in range(NRAW)]
        pair_free = [sem("pair_free0"), sem("pair_free1")]
        hi_done = sem("hi_done")
        lo_done = sem("lo_done")
        split_used = sem("split_used")
        turned = sem("turned")
        x_loaded = [sem("x_loaded0"), sem("x_loaded1")]
        consts_loaded = sem("consts_loaded")
        stacks_loaded = sem("stacks_loaded")
        tail_loaded = sem("tail_loaded")
        taps_loaded = sem("taps_loaded")
        rows_loaded = sem("rows_loaded")
        sinks_loaded = sem("sinks_loaded")
        norm_rows = sem("norm_rows")
        p_loaded = sem("p_loaded")
        stored = sem("stored")
        stack_t = sem("stack_t")
        cols_taken = sem("cols_taken")
        tail_split = sem("tail_split")
        tail_low = sem("tail_low")
        tail_out = sem("tail_out")
        tail_rows = sem("tail_rows")
        tail_turned = sem("tail_turned")
        tail_copied = sem("tail_copied")
        gates_tanh = sem("gates_tanh")
        gates_abs = sem("gates_abs")
        gates_log = sem("gates_log")
        gates_ready = sem("gates_ready")
        gate_sums = sem("gate_sums")
        gate_exp = sem("gate_exp")
        xf_done = sem("xf_done")
        xhi_done = sem("xhi_done")
        x_ready = sem("x_ready")
        p_t = sem("p_t")
        pf_done = sem("pf_done")
        p_hi_done = sem("p_hi_done")
        p_ready = sem("p_ready")
        conv_copied = sem("conv_copied")
        conv_done = sem("conv_done")
        conv_tanh = sem("conv_tanh")
        z_tanh = sem("z_tanh")
        qkv_done = sem("qkv_done")
        h_copied = sem("h_copied")
        ya_done = sem("ya_done")
        ya_hi_done = sem("ya_hi_done")
        ya_ready = sem("ya_ready")
        norm_sq = sem("norm_sq")
        norm_sum = sem("norm_sum")
        norm_rs = sem("norm_rs")
        norm_done = sem("norm_done")
        gdn_gates = sem("gdn_gates")
        gdn_products = sem("gdn_products")
        gdn_vector = sem("gdn_vector")
        gdn_exp = sem("gdn_exp")
        gdn_squares = sem("gdn_squares")
        gdn_rstd = sem("gdn_rstd")
        gdn_gated = sem("gdn_gated")
        gdn_hi = sem("gdn_hi")
        gdn_ready = sem("gdn_ready")
        r_done = sem("r_done")
        mean_done = sem("mean_done")
        rstd_done = sem("rstd_done")
        row_spread = sem("row_spread")
        z_ready = sem("z_ready")
        gate_tanh = sem("gate_tanh")
        x2_done = sem("x2_done")
        lb_diff = sem("lb_diff")
        lb_exp = sem("lb_exp")
        lb_done = sem("lb_done")
        hg_act = sem("hg_act")
        hg_gated = sem("hg_gated")
        hg_level_mm = sem("hg_level_mm")
        hg_level = sem("hg_level")
        hg_picked = sem("hg_picked")
        hg_cross_mm = sem("hg_cross_mm")
        hg_cross = sem("hg_cross")
        hg_vt = sem("hg_vt")
        hg_vt_taken = sem("hg_vt_taken")
        hg_o = sem("hg_o")
        hg_sq = sem("hg_sq")
        hg_sum = sem("hg_sum")
        hg_rs = sem("hg_rs")
        hg_y = sem("hg_y")
        hg_hi = sem("hg_hi")
        hg_ready = sem("hg_ready")
        att_in = sem("att_in")
        att_neg = sem("att_neg")
        att_exp = sem("att_exp")
        att_t = sem("att_t")
        att_pt = sem("att_pt")
        att_scale = sem("att_scale")
        att_root = sem("att_root")
        att_o = sem("att_o")
        att_hi = sem("att_hi")
        att_ready = sem("att_ready")
        relu_done = sem("relu_done")
        squared = sem("squared")
        a_hi_done = sem("a_hi_done")
        a_ready = sem("a_ready")
        final_done = sem("final_done")

        vec_chain, act_chain = sem("vec_chain"), sem("act_chain")

        def pair_of(name, i):
            return DB[PAIR[(name, i)]]

        def unit_slot(u):
            return raw[:, (u // 2) % NRAW, (u % 2) * SPLK * COLS:(u % 2 + 1) * SPLK * COLS]

        def weights(c):
            name, i, g, half = c
            k0 = (g * KT + half * RAWK) * P

            def rows(w, n=RAWK):
                return w[k0:k0 + n * P, :].rearrange("(k p) c -> p k c", p=P)

            if name == "qkvz":
                return rows(a["w_in_even"][0][:, 4 * D:8 * D]).rearrange("p k (s c) -> p k s c", s=4)[:, :, :, i * P:(i + 1) * P]
            if name == "hcbz":
                return rows(a["w_in_even"][0][:, 0:4 * D]).rearrange("p k (s c) -> p k s c", s=4)[:, :, :, i * P:(i + 1) * P]
            if name == "qfiz":
                return rows(a["w_in_odd"][0]).rearrange("p k (s c) -> p k s c", s=4)[:, :, :, i * P:(i + 1) * P]
            if name == "pl":
                return rows(a["w_pl"][i], 2)
            tensor, layer, col = {"out_even": ("w_out_even", 0, i), "out_odd": ("w_out_odd", 0, i), "gate": ("w_pl_gate", i // 2, i % 2),
                                  "q_att": ("swa_w_qkv_2", 0, i), "o_att": ("swa_w_o_2", 0, i),
                                  "up": ("mlp_w_up_2", 0, i), "down": ("mlp_w_down_2", 0, i)}[name]
            w = a[tensor][layer]
            return rows(w[:, col * COLS:(col + 1) * COLS])

        ready_at = []
        total = [0] * NRAW
        for c in LOADS:
            slot = len(ready_at) % NRAW
            total[slot] += 16 * {"kv_att": 6, "qkvz": 4, "hcbz": 4, "qfiz": 4}.get(c[0], 1)
            ready_at.append(total[slot])

        block = ctx.enter_context(nc.Block())

        @block.sync
        def _(sp):
            for c in range(2):
                for i in range(NT):
                    cols = slice(c * COLS, (c + 1) * COLS)
                    sp.dma_start(xtok[:, i, cols], a["x"][0, i * P:(i + 1) * P, cols]).then_inc(x_loaded[c], 16)
            for n, c in enumerate(LOADS):
                slot = n % NRAW
                if n == NRAW:
                    for row, name in ((CONV_A, "conv_a_w"), (LB, "lower_bounds"), (LNG, "ln_g"), (LNB, "ln_b"), (ATTN, "attn_norm_2"),
                                      (MLPN, "mlp_norm_2"), (GDNG, "gdn_norm_g"), (HGRNG, "hgrn_norm_g")):
                        src = a[name][0] if name == "conv_a_w" else a[name]
                        src = src.rearrange("k (t p) -> (k t) p", p=P)
                        sp.dma_start(GAF[row:row + src.shape[0], 1, 0:P], src).then_inc(stacks_loaded, 16)
                if n >= NRAW:
                    sp.wait_ge(lo_done, 2 * (n - NRAW + 1))
                dst = raw[:, slot, :]
                if c[0] == "kv_att":
                    w = a["swa_w_qkv_2"][0][c[3] * RAWK * P:(c[3] + 1) * RAWK * P, AH * AD:AH * AD + 2 * P]
                    w = w.rearrange("(k p) c -> p k c", p=P)
                    d = dst.rearrange("p (k c) -> p k c", k=RAWK)
                    for j in range(4):
                        sp.dma_start(d[:, :, j * AD:(j + 1) * AD], w[:, :, (j // 2) * AD:(j // 2 + 1) * AD]).then_inc(raw_ready[slot], 16)
                    for r in range(2):
                        sp.dma_start(d[:, :, (2 + r) * P:(3 + r) * P], w[:, :, P:2 * P]).then_inc(raw_ready[slot], 16)
                elif c[0] in ("qkvz", "hcbz", "qfiz"):
                    d, w = dst.rearrange("p (k s c) -> p k s c", k=RAWK, s=4), weights(c)
                    for k in range(RAWK):
                        sp.dma_start(d[:, k], w[:, k]).then_inc(raw_ready[slot], 16)
                else:
                    w = weights(c)
                    sp.dma_start(dst.rearrange("p (k c) -> p k c", k=w.shape[1]), w).then_inc(raw_ready[slot], 16)

            for i in range(NT):
                sp.wait_ge(final_done, 2 * i + 1)
                sp.dma_start(out[0, i * P:(i + 1) * P, 0:COLS], zt[:, i, 0:COLS]).then_inc(stored, 16)

        @block.gpsimd
        def _(pool):
            def scales(t):
                pool.wait_ge(att_root, t + 1)
                if t - 1 > 0:
                    pool.wait_ge(att_t, t - 1)
                pool.tensor_tensor(dg[:, t % 2, :].rearrange("p (u c) -> p u c", u=4), ident.unsqueeze(1).broadcast_to([P, 4, P]),
                                   rsum[:, t % 2, :].unsqueeze(2).broadcast_to([P, 4, P]), ALU.mult).then_inc(att_scale, 1)

            for u in range(SPLITS):
                pool.wait_ge(hi_done, u + 1)
                if u >= NSPL:
                    pool.wait_ge(split_used, u - NSPL + 1)
                pool.tensor_tensor(wlo[:, u % NSPL, :], unit_slot(u), whi[:, u % NSPL, :].bitcast(F32),
                                   ALU.subtract).then_inc(lo_done, 1)
                beside = u - FIRST_SPLIT[("q_att", 1, 0)] - AHEAD
                if 1 <= beside < 3:
                    scales(beside - 1)
                if beside == 3:
                    for t in range(2, 8):
                        scales(t)

        @block.tensor
        def _(pe):
            at = {"unit": 0}

            def group_start(name, i):
                if BEFORE[(name, i)] > 0:
                    pe.wait_ge(pair_free[PAIR[(name, i)]], BEFORE[(name, i)])

            def three(out_, lw, rw, start, stop, l_cols=None):
                (lh, ll), (rh, rl_) = lw, rw
                pe.matmul(out_, lh, rh, start=start, stop=False, skip_group_check=True)
                pe.matmul(out_, lh, rl_, start=False, stop=False, skip_group_check=True)
                return pe.matmul(out_, ll, rh, start=False, stop=stop, skip_group_check=True)

            def unit_ready():
                u = at["unit"]
                pe.wait_ge(lo_done, u + 1)
                at["unit"] += 1
                slot = u % NSPL
                return (whi[:, slot, :].rearrange("p (k c) -> p k c", k=SPLK), wlo[:, slot, :].rearrange("p (k c) -> p k c", k=SPLK))

            def feature_unit(name, i, q, xh, xl, tiles=4):
                if q == 0:
                    group_start(name, i)
                wh, wl = unit_ready()
                bank = pair_of(name, i)
                for kk in range(SPLK):
                    k = q * SPLK + kk
                    for t in range(tiles):
                        cols = slice(t * P, (t + 1) * P)
                        last = three(bank[t // 2][:, (t % 2) * T:(t % 2 + 1) * T], (wh[:, kk, cols], wl[:, kk, cols]),
                                     (xh[:, k, :], xl[:, k, :]), start=(k == 0 and t % 2 == 0), stop=(k == KT - 1))
                return last

            def token_unit(name, i, q, xh, xl, start, stop):
                wh, wl = unit_ready()
                bank = pair_of(name, i)
                for kk in range(SPLK):
                    k = q * SPLK + kk
                    for t in range(NT):
                        tok = slice(t * P, (t + 1) * P)
                        last = three(bank[t][:, :], (xh[:, k, tok], xl[:, k, tok]), (wh[:, kk, :], wl[:, kk, :]),
                                     start=start and kk == 0, stop=stop and kk == SPLK - 1)
                return last

            def dense_feature(name, i, q, xh, xl):
                feature_unit(name, i, q, xh, xl).then_inc(split_used, 1)

            def transposes(name, first, src, source_ready, counts, halves=range(2)):
                for c in halves:
                    pe.wait_ge(source_ready, counts[c])
                    group_start(name, first + c)
                    bank = pair_of(name, first + c)
                    for b in range(2):
                        for j in range(2):
                            for t in range(NT):
                                k = 4 * c + 2 * b + j
                                last = pe.transpose(bank[b][:, j * T + t * P:j * T + (t + 1) * P], src[:, t, k * P:(k + 1) * P], ident)
                    last.then_inc(turned, 1)

            def layer_tail(layer):
                pe.wait_ge(p_ready, layer + 1)
                for k in range(2):
                    wh, wl = unit_ready()
                    for t in range(NT):
                        tok = slice(t * P, (t + 1) * P)
                        for c in range(2):
                            cols = slice(c * COLS, (c + 1) * COLS)
                            w = [x[:, :, :].rearrange("p k c -> p (k c)")[:, cols] for x in (wh, wl)]
                            last = three(SB[2 * t + c][:, :], (p_hi[:, k, tok], p_lo[:, k, tok]), w, start=(k == 0), stop=(k == 1))
                    last.then_inc(split_used, 1)
                transposes("ln_t", 2 * layer, zt, z_ready, [4 * layer + 2, 4 * layer + 4])
                for c in range(2):
                    group_start("gate", 2 * layer + c)
                    for q in range(4):
                        pe.wait_ge(x_ready, 4 + 8 * layer + q + 1)
                        token_unit("gate", 2 * layer + c, q, ya_hi, ya_lo, q == 0, q == 3).then_inc(split_used, 1)
                        if c == 1 and q == 1:
                            transposes(("x2_t", "att_t")[layer], 0, xtok, x2_done, [2 * layer + 1], range(1))

            def p_transposes(layer):
                pe.wait_ge(p_loaded, 16 * (layer + 1))
                for k in range(2):
                    for t in range(NT):
                        last = pe.transpose(SB[0][:, k * T + t * P:k * T + (t + 1) * P], ptk[:, t, k * P:(k + 1) * P], ident)
                last.then_inc(p_t, 1)

            pe.wait_ge(consts_loaded, 16)
            transposes("x_t", 0, xtok, x_loaded[0], [32, 32], range(1))

            def tail():
                pe.wait_ge(tail_low, 1)
                for k in range(KT):
                    last = three(SB[1][0:16, 0:T], (tail_hi[:, k, :], tail_lo[:, k, :]), (x_hi[:, k, :], x_lo[:, k, :]),
                                 start=(k == 0), stop=(k == KT - 1))
                last.then_inc(tail_out, 1)

            def tail_turn():
                pe.wait_ge(tail_rows, 1)
                for t in range(NT):
                    last = pe.transpose(SB[1][:, T + 16 * t:T + 16 * t + 16], hs[0:16, t * P:(t + 1) * P], ident[0:16, 0:16])
                last.then_inc(tail_turned, 1)

            def norm_sum_of(h):
                pe.wait_ge(norm_sq, h + 1)
                if h == 0:
                    pe.wait_ge(cols_taken, 1)
                if h == 2:
                    pe.wait_ge(cols_taken, 2)
                if h == 1:
                    pe.wait_ge(tail_copied, 1)
                if h == 3:
                    pe.wait_ge(gate_exp, 1)
                if h >= 4:
                    pe.wait_ge(norm_rs, h - 3)
                pe.matmul(SB[h % 4][:, :], ones, EL[:, h % 2, :], start=True, stop=True).then_inc(norm_sum, 1)

            for h in range(GH):
                for q in range(4):
                    if h == 0:
                        pe.wait_ge(x_ready, q + 1)
                    dense_feature("qkvz", h, q, x_hi, x_lo)
                    if h == 1 and q == 0:
                        tail_turn()
                    if h == 0 and q == 0:
                        transposes("x_t", 0, xtok, x_loaded[1], [32, 32], range(1, 2))
                    if h == 0 and q == 3:
                        pe.wait_ge(taps_loaded, 16)
                        pe.transpose(SB[0][:, 0:STACK_A], stA, ident[0:STACK_A, 0:STACK_A]).then_inc(stack_t, 1)
                    if h == 2 and q == 3:
                        pe.wait_ge(stacks_loaded, 128)
                        pe.transpose(SB[2][:, 0:STACK_B], stB, ident[0:STACK_B, 0:STACK_B]).then_inc(stack_t, 1)
                    if h >= 2 and q == 1:
                        norm_sum_of(h - 2)
                if h == 0:
                    tail()
                if h == 2:
                    pe.wait_ge(gates_ready, 1)
                    pe.matmul(SB[3][:, 0:GH], after, gt[:, 5, 0, :], start=True, stop=True)
                    pe.matmul(SB[3][:, GH:2 * GH], upto, gt[:, 5, 1, :], start=True, stop=True).then_inc(gate_sums, 1)

            def unit(g_buf, u):
                return g_buf[:, u * P:(u + 1) * P]

            def even_odd(ap, s, which):
                return ap.rearrange("p (m t r) -> p m t r", t=2, r=s)[:, :, which, :]

            def gdn(half, s):
                for g in range(2):
                    if (s, g) not in PE_STEPS:
                        continue
                    A, B = SB[2 * g], SB[2 * g + 1]
                    tok = slice(g * P, (g + 1) * P)
                    heads = [4 * half + u for u in range(4)]
                    if s == 0:
                        pe.wait_ge(gdn_gates, half + 1)
                        if half == 0:
                            pe.wait_ge(norm_rs, GH)
                        else:
                            pe.wait_ge(gdn_vector, dve_step(0, 20, g))
                    elif s == 1:
                        pe.wait_ge(norm_done, 4 * half + 4)
                        pe.wait_ge(gdn_vector, dve_step(half, 0, g))
                    elif s < 17:
                        pe.wait_ge(gdn_vector, dve_step(half, s - 1, g))
                    elif s == 17:
                        pe.wait_ge(gdn_vector, dve_step(half, 16, 0))
                    elif s == 18:
                        pe.wait_ge(gdn_vector, dve_step(half, 17, 0))
                    elif s == 19:
                        pe.wait_ge(gdn_vector, dve_step(half, 18, 1))
                    else:
                        pe.wait_ge(gdn_squares, 2 * half + g + 1)
                    for u, h in enumerate(heads):
                        o = slice(u * P, (u + 1) * P)
                        if s == 0:
                            pe.matmul(A[:, o], upto, unit(GAF[:, g, :], u), start=True, stop=True)
                            last = pe.matmul(B[:, o], unit(GAF[:, g, :], u), upto, start=True, stop=True)
                        elif s == 1:
                            pe.matmul(A[:, o], kT[:, h, tok], kT[:, h, tok], start=True, stop=True)
                            last = pe.matmul(B[:, o], kT[:, h, tok], qT[:, h, tok], start=True, stop=True)
                        elif s == 2:
                            last = pe.transpose(A[:, o], unit(EL[:, g, :], u), ident)
                            if g == 1:
                                last = pe.matmul(B[:, o], gt[:, 5, 1, h:h + 1].broadcast_to([P, P]), upto, start=True, stop=True)
                        elif s == 3:
                            pe.transpose(A[:, o], kT[:, h, tok], ident)
                            last = pe.transpose(B[:, o], vT[:, h, tok], ident)
                        elif s < 16 and s % 2 == 0:
                            last = pe.matmul(A[:, o], unit(LT[:, g, :], u), unit(XN[:, g, :], u), start=True, stop=True)
                        elif s < 16:
                            lv = LEVELS[(s - 5) // 2 + 1]
                            if s != 15:
                                pe.matmul(B[:, u * 64:(u + 1) * 64], unit(XT[:, g, :], u), even_odd(unit(EL[:, g, :], u), lv, 0), start=True, stop=True)
                            last = pe.matmul(B[:, 256 + u * 64:256 + (u + 1) * 64], unit(EL[:, g, :], u), even_odd(unit(XT[:, g, :], u), lv, 1),
                                             start=True, stop=True)
                        elif s == 16 and g == 0:
                            last = pe.matmul(A[:, o], unit(XT[:, 0, :], u), unit(VB[:, 0, :], u), start=True, stop=True)
                        elif s == 16:
                            last = pe.matmul(A[:, o], unit(KX[:, 1, :], u), unit(XT[:, 1, :], u), start=True, stop=True)
                        elif s == 17:
                            last = pe.matmul(B[:, o], unit(KX[:, 0, :], u), unit(XN[:, 0, :], u), start=True, stop=True)
                        elif s == 18:
                            pe.matmul(A[:, o], unit(XT[:, 1, :], u), unit(VB[:, 1, :], u), start=True, stop=False)
                            last = pe.matmul(A[:, o], unit(LT[:, 1, :], u), unit(LT[:, 0, :], u), start=False, stop=True)
                    if s == 19:
                        for j in range(2):
                            u = 2 * g + j
                            pe.matmul(A[:, j * T:j * T + P], unit(XN[:, 0, :], u), unit(AT[:, 0, :], u), start=True, stop=True)
                            pe.matmul(A[:, j * T + P:(j + 1) * T], unit(LT[:, 0, :], u), unit(QD[:, 1, :], u), start=True, stop=False)
                            last = pe.matmul(A[:, j * T + P:(j + 1) * T], unit(XN[:, 1, :], u), unit(AT[:, 1, :], u), start=False, stop=True)
                    if s == 20:
                        last = pe.matmul(B[:, :], ones, EL[:, g, :], start=True, stop=True)
                    last.then_inc(gdn_products, 1)

            def out_unit(name, n):
                g = n // 8
                c, q = (n // 4 % 2, n % 4) if g == 0 else (n // 2 % 2, n % 2 + 2 * (n // 4 % 2))
                if g == 0 and q == 0:
                    group_start(name, c)
                xh, xl = ((ya_hi, ya_lo), (yb_hi, yb_lo))[g]
                if name == "out_even":
                    pe.wait_ge(ya_ready if g == 0 else gdn_ready, 2 * q + 2 if g == 0 else q + 1)
                else:
                    pe.wait_ge(hg_ready, 4 * g + q + 1)
                token_unit(name, c, q, xh, xl, g == 0 and q == 0, g == 1 and q == 3).then_inc(split_used, 1)

            def beside(n):
                if n < 4 * KT:
                    dense_feature("hcbz", n // 4, n % 4, x_hi, x_lo)
                elif n < BESIDE:
                    out_unit("out_even", n - 4 * KT)

            for n in range(LEAD):
                beside(n)
                if n == 1:
                    norm_sum_of(GH - 2)
            norm_sum_of(GH - 1)
            for half in range(2):
                for s in range(GSTEPS):
                    beside(LEAD + half * GSTEPS + s)
                    gdn(half, s)
            for n in range(BESIDE - 4 * KT, 16):
                if n == 15:
                    p_transposes(0)
                out_unit("out_even", n)
            layer_tail(0)

            def hg_unit(buf, par, i, t):
                return buf[:, par, i * T + t * P:i * T + (t + 1) * P]

            for it in range(HH // 2 + 2):
                L, C = it - 1, it - 2
                pl_, pc = L % 2, C % 2
                for k in range(8):
                    if it < HH // 2:
                        if it == 0:
                            pe.wait_ge(x_ready, 8 + k % 4 + 1)
                        dense_feature("qfiz", 2 * it + k // 4, k % 4, x_hi, x_lo)
                        if it == 0 and k == 0:
                            transposes("x2_t", 0, xtok, x2_done, [1, 2], range(1, 2))
                    else:
                        out_unit("out_odd", (it - HH // 2) * 8 + k)
                    if k == 0 and 0 <= C < HH // 2:
                        pe.wait_ge(hg_level, 7 * C + 7)
                        pe.wait_ge(hg_picked, 7 * C + 6)
                        for i in range(2):
                            last = pe.matmul(SB[0][:, i * P:(i + 1) * P], hg_unit(KS, pc, i, 0), hg_unit(QS, pc, i, 1), start=True, stop=True)
                        last.then_inc(hg_cross_mm, 1)
                    if k == 0 and 0 <= L < HH // 2:
                        pe.wait_ge(hg_act, 2 * L + 2)
                        if C > 0:
                            pe.wait_ge(hg_rs, C)
                        for i in range(2):
                            for t in range(NT):
                                last = pe.transpose(SB[2][:, (2 * i + t) * P:(2 * i + t + 1) * P], vfm[:, pl_, i, t * P:(t + 1) * P], ident)
                        last.then_inc(hg_vt, 1)
                    if k >= 1 and 0 <= L < HH // 2:
                        if k == 1:
                            pe.wait_ge(hg_gated, 2 * L + 2)
                            pe.wait_ge(hg_cross, C + 1)
                            if L > 0:
                                pe.wait_ge(hg_picked, 7 * L)
                        else:
                            pe.wait_ge(hg_level, 7 * L + k - 1)
                            pe.wait_ge(hg_picked, 7 * L + max(k - 2, 1))
                        s = LEVELS[k - 1]
                        for i in range(2):
                            for t in range(NT):
                                u = 2 * i + t
                                if k == 1:
                                    pe.matmul(SB[0][:, u * P:(u + 1) * P], hg_unit(KS, pl_, i, t), hg_unit(q0, pl_, i, t), start=True, stop=True)
                                last = pe.matmul(SB[k % 2][:, u * 64:(u + 1) * 64], hg_unit(KS, pl_, i, t), even_odd(hg_unit(QS, pl_, i, t), s, 1),
                                                 start=True, stop=True)
                        last.then_inc(hg_level_mm, 1)
                    if k == 1 and 0 <= C < HH // 2:
                        pe.wait_ge(hg_picked, 7 * C + 7)
                        pe.wait_ge(hg_cross, C + 1)
                        pe.wait_ge(hg_vt_taken, C + 1)
                        if C > 0:
                            pe.wait_ge(hg_y, C)
                        for i in range(2):
                            v0, v1 = unit(vtok[:, pc, :], 2 * i), unit(vtok[:, pc, :], 2 * i + 1)
                            pe.matmul(SB[3][:, i * T:i * T + P], v0, unit(AA[:, pc, :], 2 * i), start=True, stop=True)
                            pe.matmul(SB[3][:, i * T + P:(i + 1) * T], v0, unit(CR[:, pc, :], i), start=True, stop=False)
                            last = pe.matmul(SB[3][:, i * T + P:(i + 1) * T], v1, unit(AA[:, pc, :], 2 * i + 1), start=False, stop=True)
                        last.then_inc(hg_o, 1)
                    if k == 2 and 0 <= C < HH // 2:
                        pe.wait_ge(hg_sq, C + 1)
                        pe.wait_ge(hg_vt_taken, min(L + 1, HH // 2))
                        pe.matmul(SB[2][:, :], ones, sqo[:, :], start=True, stop=True).then_inc(hg_sum, 1)
                    if it == HH // 2 + 1 and k == 6:
                        p_transposes(1)
            layer_tail(1)

            def root_row():
                for i in range(NT):
                    last = pe.matmul(SB[0][:, i * P:(i + 1) * P], mv[:, i, 2:3].broadcast_to([P, P]), ident, start=True, stop=True)
                last.then_inc(row_spread, 1)

            for q in range(4):
                pe.wait_ge(x_ready, 16 + q + 1)
                dense_feature("q_att", 0, q, x_hi, x_lo)
                if q == 0:
                    transposes("att_t", 0, xtok, x2_done, [3, 4], range(1, 2))
            pe.wait_ge(rstd_done, 3)
            root_row()
            group_start("kv_att", 0)
            bank = pair_of("kv_att", 0)
            for q in range(4):
                wh, wl = unit_ready()
                for kk in range(SPLK):
                    k = q * SPLK + kk
                    for t in range(2):
                        cols = slice(t * P, (t + 1) * P)
                        three(bank[0][:, t * T:(t + 1) * T], (wh[:, kk, cols], wl[:, kk, cols]), (x_hi[:, k, :], x_lo[:, k, :]),
                              start=(k == 0 and t == 0), stop=(k == KT - 1))
                        last = three(bank[1][:, t * P:(t + 1) * P], (x_hi[:, k, cols], x_lo[:, k, cols]),
                                     (wh[:, kk, 2 * P:3 * P], wl[:, kk, 2 * P:3 * P]), start=(k == 0 and t == 0), stop=(k == KT - 1))
                last.then_inc(split_used, 1)

            def o_unit(c, q):
                if q == 0:
                    group_start("o_att", c)
                pe.wait_ge(att_ready, 2 * q + 2)
                token_unit("o_att", c, q, ya_hi, ya_lo, q == 0, q == 3).then_inc(split_used, 1)

            dense_feature("q_att", 1, 0, x_hi, x_lo)
            for t in range(11):
                if t < 8:
                    if t == 0:
                        pe.wait_ge(att_in, 4)
                    if t == 4:
                        pe.wait_ge(att_in, 6)
                    group_start("score", t)
                    bank = pair_of("score", t)
                    for j in range(2):
                        part = slice(j * AD, (j + 1) * AD)
                        pe.matmul(bank[j][:, 0:T], qa[part, t, P:T], ka[part, t // 4, :], start=True, stop=True)
                        last = pe.matmul(bank[j][:, T:T + P], qa[part, t, 0:P], ka[part, t // 4, 0:P], start=True, stop=True)
                    last.then_inc(turned, 1)
                if t < 3:
                    dense_feature("q_att", 1, t + 1, x_hi, x_lo)
                if t == 6:
                    o_unit(0, 0)
                if t in (8, 9):
                    o_unit(t - 8, 9 - t)
                if 2 <= t < 10:
                    r = t - 2
                    pe.wait_ge(att_exp, r + 1)
                    pe.wait_ge(att_scale, r + 1)
                    if r > 0:
                        pe.wait_ge(att_pt, r)
                    for j in range(6):
                        b = SB[2][:, j * P:(j + 1) * P] if j < 4 else SB[3][:, (j - 4) * P:(j - 3) * P]
                        head, tile, block = (j // 2, 0, j % 2) if j < 4 else (j - 4, 1, 2)
                        last = pe.matmul(b, lg[:, r % 3, (3 * head + block) * P:(3 * head + block + 1) * P],
                                         dg[:, r % 2, (2 * tile + head) * P:(2 * tile + head + 1) * P], start=True, stop=True)
                    last.then_inc(att_t, 1)
                if t >= 3:
                    r = t - 3
                    pe.wait_ge(att_pt, r + 1)
                    if r - 1 > 0:
                        pe.wait_ge(att_ready, r - 1)
                    v = slice((r // 4) * AD, (r // 4 + 1) * AD)
                    for j in range(2):
                        part = slice(j * AD, (j + 1) * AD)
                        probs = pt[:, r % 2, :]
                        pe.matmul(SB[r % 2][part, 0:P], va[:, 0, v], probs[:, (4 + j) * P:(5 + j) * P], start=True, stop=True)
                        pe.matmul(SB[r % 2][part, P:T], va[:, 0, v], probs[:, 2 * j * P:(2 * j + 1) * P], start=True, stop=False)
                        last = pe.matmul(SB[r % 2][part, P:T], va[:, 1, v], probs[:, (2 * j + 1) * P:(2 * j + 2) * P], start=False, stop=True)
                    last.then_inc(att_o, 1)
            for c, q in ((1, 1), (0, 2), (0, 3), (1, 2), (1, 3)):
                o_unit(c, q)
                if (c, q) == (1, 2):
                    transposes("mlp_t", 0, xtok, r_done, [10], range(1))

            for c in range(8):
                for q in range(4):
                    if c == 0:
                        pe.wait_ge(x_ready, 20 + q + 1)
                    dense_feature("up", c, q, x_hi, x_lo)
                    if c == 0 and q == 0:
                        transposes("mlp_t", 0, xtok, r_done, [10, 12], range(1, 2))
                if c == 0:
                    pe.wait_ge(rstd_done, 4)
                    root_row()
            for g in range(4):
                for c in range(2):
                    if g == 0:
                        group_start("down", c)
                    for q in range(4):
                        ch = (8 * g + 2 * q) // 4
                        pe.wait_ge(a_ready, ch + 1)
                        ah, al = act_tiles(ch)
                        wh, wl = unit_ready()
                        bank = pair_of("down", c)
                        for kk in range(SPLK):
                            for t in range(NT):
                                tok = slice(t * P, (t + 1) * P)
                                k = 2 * (q % 2) + kk
                                last = three(bank[t][:, :], (ah[:, k, tok], al[:, k, tok]), (wh[:, kk, :], wl[:, kk, :]),
                                             start=(g == 0 and q == 0 and kk == 0), stop=(g == 3 and q == 3 and kk == 1))
                        last.then_inc(split_used, 1)

        @block.scalar
        def _(act):
            raised = {}
            at = {"unit": 0}

            def link(ins, sem_=act_chain):
                ins.then_inc(sem_, 1)
                settle(sem_)

            def settle(sem_):
                raised[id(sem_)] = raised.get(id(sem_), 0) + 1
                act.wait_ge(sem_, raised[id(sem_)])

            def tables(name):
                if at.get("tables") != name:
                    at["tables"] = name
                    act.preload_act_table_set(name)

            def split_until(end):
                while at["unit"] < min(end, SPLITS):
                    u = at["unit"]
                    act.wait_ge(raw_ready[(u // 2) % NRAW], ready_at[u // 2])
                    if u >= NSPL:
                        act.wait_ge(split_used, u - NSPL + 1)
                        act.wait_ge(lo_done, u - NSPL + 1)
                    act.activation(whi[:, u % NSPL, :], unit_slot(u), ACT.Copy).then_inc(hi_done, 1)
                    at["unit"] += 1

            def group_ready(name, i):
                if (name, i) in UNITS_DONE:
                    act.wait_ge(split_used, UNITS_DONE[(name, i)])
                else:
                    act.wait_ge(turned, TURNED[(name, i)])

            def take_hi(src, hi, base, parts=range(4)):
                for b in parts:
                    act.wait_ge(xf_done, base + b + 1)
                    act.activation(hi[:, 2 * b:2 * b + 2, :], src[:, b % 2, :].rearrange("p (k t) -> p k t", k=2), ACT.Copy).then_inc(xhi_done, 1)
                    settle(xhi_done)

            def take_p(layer):
                act.wait_ge(pf_done, layer + 1)
                act.activation(p_hi[:, :, :], pf[:, :, :], ACT.Copy).then_inc(p_hi_done, 1)
                settle(p_hi_done)

            def load_rows(layer):
                act.dma_start(ptk[:, :, :], a["p"][layer, 0].rearrange("(t p) c -> p t c", p=P)).then_inc(p_loaded, 16)
                act.dma_start(gb[:, 0, :], a["ln_g"][layer:layer + 1, :].broadcast_to([P, D])).then_inc(norm_rows, 16)
                act.dma_start(gb[:, 1, :], a["ln_b"][layer:layer + 1, :].broadcast_to([P, D])).then_inc(norm_rows, 16)

            def rstd(n, eps):
                tables(LOG_TABLES)
                act.wait_ge(mean_done, n + 1)
                link(act.activation(mv[:, :, 2:3], mv[:, :, 1:2], ACT.Ln, bias=eps))
                act.activation(mv[:, :, 2:3], mv[:, :, 2:3], ACT.Exp, scale=-0.5).then_inc(rstd_done, 1)
                settle(rstd_done)

            act.dma_start(con[:, 0:C_NEG], consts[:, 0:C_NEG]).then_inc(consts_loaded, 16)
            act.dma_start(tail_w[:, :, :], a["w_in_even"][0][:, 8 * D:8 * D + 16].rearrange("(k p) c -> p k c", p=P)).then_inc(tail_loaded, 16)
            act.dma_start(stA, a["conv_b_w"][0].rearrange("k (t p) -> (k t) p", p=P)).then_inc(taps_loaded, 16)
            act.dma_start(gate_rows[:, 0, :], a["a_log"][0:1, :].broadcast_to([P, GH])).then_inc(rows_loaded, 16)
            act.dma_start(gate_rows[:, 1, :], a["dt_bias"][0:1, :].broadcast_to([P, GH])).then_inc(rows_loaded, 16)
            tables(EXP_TABLES)
            take_hi(xf0, x_hi, 0, range(2))
            split_until(3)
            take_hi(xf0, x_hi, 0, range(2, 4))
            split_until(AHEAD)
            act.dma_start(con[:, C_NEG:], consts[:, C_NEG:]).then_inc(consts_loaded, 16)
            act.wait_ge(tail_loaded, 16)
            act.activation(tail_hi[:, :, :], tail_w[:, :, :], ACT.Copy).then_inc(tail_split, 1)
            settle(tail_split)

            def gates():
                act.wait_ge(tail_turned, 1)
                act.activation(gt[:, 0:2, :, :].rearrange("p s t h -> p t s h"),
                    SB[1][:, T:T + 32].rearrange("p (t s h) -> p t s h", t=2, s=2), ACT.Copy).then_inc(tail_copied, 1)
                settle(tail_copied)
                link(act.activation(gt[:, 2, :, :], gt[:, 0, :, :], ACT.Tanh, scale=0.5))
                act.wait_ge(rows_loaded, 32)
                act.activation(gate_rows[:, 0, :], gate_rows[:, 0, :], ACT.Exp).then_inc(gates_tanh, 1)
                settle(gates_tanh)
                act.wait_ge(gates_abs, 1)
                tables(LOG_TABLES)
                link(act.activation(gt[:, 4, :, :], gt[:, 4, :, :], ACT.Exp))
                act.activation(gt[:, 4, :, :], gt[:, 4, :, :], ACT.Ln, bias=1.0).then_inc(gates_log, 1)
                settle(gates_log)
                tables(EXP_TABLES)

            def root_of(h):
                return (XN, XT)[h % 4 // 2][:, h % 2, :]

            def norm_squares(h):
                act.wait_ge(qkv_done, h + 1)
                if h >= 2:
                    act.wait_ge(norm_sum, h - 1)
                act.activation(EL[:, h % 2, 0:T], qT[:, h, :], ACT.Square).then_inc(act_chain, 1)
                settle(act_chain)
                act.activation(EL[:, h % 2, T:2 * T], kT[:, h, :], ACT.Square).then_inc(norm_sq, 1)
                settle(norm_sq)

            def norm_root(h):
                act.wait_ge(norm_sum, h + 1)
                if h >= 4:
                    act.wait_ge(norm_done, h - 3)
                link(act.activation(root_of(h), SB[h % 4][:, :], ACT.Ln, bias=4e-6))
                act.activation(root_of(h), root_of(h), ACT.Exp, scale=-0.5).then_inc(norm_rs, 1)
                settle(norm_rs)

            for h in range(GH):
                split_until(FIRST_SPLIT[("qkvz", h, 0)] + 3 + AHEAD)
                if h == 1:
                    gates()
                group_ready("qkvz", h)
                bank = pair_of("qkvz", h)
                if h > 0:
                    act.wait_ge(conv_done, h)
                act.activation(pad[:, 0:2, 3:T + 3], bank[0][:, :].rearrange("p (s t) -> p s t", s=2), ACT.Copy).then_inc(conv_copied, 1)
                settle(conv_copied)
                act.activation(pad[:, 2, 3:T + 3], bank[1][:, 0:T], ACT.Copy).then_inc(conv_copied, 1)
                settle(conv_copied)
                if h > 0:
                    act.wait_ge(qkv_done, h)
                act.activation(thz[:, :], bank[1][:, T:2 * T], ACT.Tanh, scale=0.5).then_inc(z_tanh, 1)
                settle(z_tanh)
                if h == 0:
                    act.wait_ge(tail_out, 1)
                    act.activation(hs[0:16, :], SB[1][0:16, 0:T], ACT.Copy).then_inc(tail_rows, 1)
                    settle(tail_rows)
                if h >= 1:
                    norm_squares(h - 1)
                if h == 3:
                    act.wait_ge(gate_sums, 1)
                    act.activation(gt[:, 6, :, :], SB[3][:, 0:2 * GH].rearrange("p (t h) -> p t h", t=2), ACT.Exp).then_inc(gate_exp, 1)
                    settle(gate_exp)
                if h >= 5:
                    tables(LOG_TABLES)
                    norm_root(2 * h - 10)
                    norm_root(2 * h - 9)
                    tables(EXP_TABLES)
                if h == GH - 1:
                    split_until(FIRST_SPLIT[("hcbz", 0, 0)] + 2 + AHEAD)
                act.wait_ge(conv_done, h + 1)
                act.activation(th, cv, ACT.Tanh, scale=0.5).then_inc(conv_tanh, 1)
                settle(conv_tanh)
            split_until(FIRST_SPLIT[("hcbz", 0, 0)] + 3 + AHEAD)
            norm_squares(GH - 1)
            tables(LOG_TABLES)
            norm_root(6)
            norm_root(7)

            def gdn(half, s):
                for g in range(2):
                    A, B = SB[2 * g], SB[2 * g + 1]
                    if s == 0:
                        act.wait_ge(gdn_products, pe_step(half, 0, g))
                        link(act.activation(EL[:, g, :], A[:, :], ACT.Exp))
                        act.activation(AT[:, g, :], B[:, :], ACT.Exp).then_inc(gdn_exp, 1)
                        settle(gdn_exp)
                    if s == 2 and g == 1:
                        act.wait_ge(gdn_products, pe_step(half, 2, 1))
                        act.activation(QD[:, 0, :], B[:, :], ACT.Exp).then_inc(gdn_exp, 1)
                        settle(gdn_exp)
                    if s == 18:
                        tables(LOG_TABLES)
                    if s == 19:
                        act.wait_ge(gdn_products, pe_step(half, 19, g))
                        act.activation(EL[:, g, :], A[:, :], ACT.Square).then_inc(gdn_squares, 1)
                        settle(gdn_squares)
                    if s == 20:
                        act.wait_ge(gdn_products, pe_step(half, 20, g))
                        link(act.activation(KX[:, g, :], B[:, :], ACT.Ln, scale=1.0 / P, bias=EPS))
                        act.activation(KX[:, g, :], KX[:, g, :], ACT.Exp, scale=-0.5).then_inc(gdn_rstd, 1)
                        settle(gdn_rstd)
                if s == 20:
                    for g in range(2):
                        act.wait_ge(gdn_gated, 2 * half + g + 1)
                        hh = 4 * half + 2 * g
                        act.activation(yb_hi[:, hh:hh + 2, :], VB[:, g, :].rearrange("p (h t) -> p h t", h=2), ACT.Copy).then_inc(gdn_hi, 1)
                        settle(gdn_hi)

            def ya(j):
                group_ready("hcbz", j)
                bank = pair_of("hcbz", j)
                if j > 0:
                    act.wait_ge(ya_done, j)
                act.wait_ge(qkv_done, GH)
                act.activation(hs[:, :], bank[0][:, 0:T], ACT.Copy).then_inc(h_copied, 1)
                settle(h_copied)
                tables(EXP_TABLES)
                act.activation(thz[:, :], bank[1][:, T:2 * T], ACT.Tanh, scale=0.5).then_inc(h_copied, 1)
                settle(h_copied)

            def ya_high(j):
                act.wait_ge(ya_done, j + 1)
                act.activation(ya_hi[:, j, :], yf[:, :], ACT.Copy).then_inc(ya_hi_done, 1)
                settle(ya_hi_done)

            for half in range(2):
                for s in range(GSTEPS):
                    slot = half * GSTEPS + s
                    split_until(FIRST_SPLIT[("hcbz", 0, 0)] + min(slot + LEAD + 1, BESIDE) + AHEAD)
                    gdn(half, s)
                    if slot < 32 and slot % 4 == 0:
                        ya(slot // 4)
                    if slot < 32 and slot % 4 == 1:
                        ya_high(slot // 4)

            def layer_end(layer):
                load_rows(layer)
                split_until(FIRST_SPLIT[("pl", layer, 0)] + 2)
                take_p(layer)
                split_until(FIRST_SPLIT[("gate", 2 * layer, 0)] + AHEAD)
                rstd(layer, EPS)
                take_hi(xf, ya_hi, 4 + 8 * layer)
                tables(EXP_TABLES)
                for c in range(2):
                    if c == 1:
                        split_until(FIRST_SPLIT[("gate", 2 * layer + 1, 0)] + 2 + AHEAD)
                        take_hi(xf, x_hi, 8 + 8 * layer, range(2))
                    split_until(FIRST_SPLIT[("gate", 2 * layer + c, 0)] + 4 + AHEAD)
                    group_ready("gate", 2 * layer + c)
                    bank = pair_of("gate", 2 * layer + c)
                    if 2 * layer + c > 0:
                        act.wait_ge(x2_done, 2 * layer + c)
                    for i in range(NT):
                        act.activation(eg[:, i, :], bank[i][:, :], ACT.Tanh, scale=0.5).then_inc(gate_tanh, 1)
                        settle(gate_tanh)

            act.wait_ge(gdn_ready, 4)
            act.wait_ge(ya_ready, KT)
            layer_end(0)
            take_hi(xf, x_hi, 8, range(2, 4))

            act.wait_ge(lb_diff, 1)
            act.activation(lbc[:, 0:2, :], lbc[:, 0:2, :], ACT.Exp).then_inc(lb_exp, 1)
            settle(lb_exp)

            def hg_dense(h):
                p, i = h // 2, h % 2
                group_ready("qfiz", h)
                bank = pair_of("qfiz", h)
                if h - 1 > 0:
                    act.wait_ge(hg_gated, h - 1)
                if p - 1 > 0:
                    act.wait_ge(hg_vt, p - 1)
                link(act.activation(qfth[:, i, :], bank[0][:, :], ACT.Tanh, scale=0.5))
                link(act.activation(zth[:, i, :], bank[1][:, T:2 * T], ACT.Tanh, scale=0.5))
                act.activation(vfm[:, p % 2, i, :], bank[1][:, 0:T], ACT.Copy).then_inc(hg_act, 1)
                settle(hg_act)

            for it in range(HH // 2 + 2):
                C = it - 2
                for k in range(8):
                    if it < HH // 2:
                        split_until(FIRST_SPLIT[("qfiz", 2 * it, 0)] + k + 1 + AHEAD)
                    elif it == HH // 2:
                        split_until(FIRST_SPLIT[("out_odd", 0, 0)] + k + 1 + AHEAD)
                    elif k < 3:
                        split_until(FIRST_SPLIT[("out_odd", 0, 1)] + k + 1 + AHEAD)
                    if k == 0 and 0 < it <= HH // 2:
                        hg_dense(2 * it - 1)
                    if k == 4 and it < HH // 2:
                        hg_dense(2 * it)
                    if 0 <= C < HH // 2:
                        if k == 1:
                            act.wait_ge(hg_o, C + 1)
                            act.activation(sqo[:, :], SB[3][:, :], ACT.Square).then_inc(hg_sq, 1)
                            settle(hg_sq)
                        if k == 2:
                            act.wait_ge(hg_sum, C + 1)
                            if C > 0:
                                act.wait_ge(hg_y, C)
                            tables(LOG_TABLES)
                            link(act.activation(rso[:, :], SB[2][:, :], ACT.Ln, scale=1.0 / P, bias=4 * EPS))
                            act.activation(rso[:, :], rso[:, :], ACT.Exp, scale=-0.5).then_inc(hg_rs, 1)
                            settle(hg_rs)
                            tables(EXP_TABLES)
                        if k == 3:
                            act.wait_ge(hg_y, C + 1)
                            hi = (ya_hi, yb_hi)[C // 4]
                            act.activation(hi[:, 2 * (C % 4):2 * (C % 4) + 2, :], yo[:, :].rearrange("p (h t) -> p h t", h=2),
                                ACT.Copy).then_inc(hg_hi, 1)
                            settle(hg_hi)
            act.wait_ge(hg_ready, HH // 2)
            layer_end(1)

            take_hi(xf, x_hi, 16, range(2, 4))
            split_until(FIRST_SPLIT[("q_att", 0, 0)] + 1 + AHEAD)
            rstd(2, RMS_EPS)
            act.dma_start(sink_row[:, :], a["swa_sinks_2"][0:1, :].broadcast_to([P, AH])).then_inc(sinks_loaded, 16)
            act.dma_start(gb[:, 0, :], a["final_norm_2"].rearrange("(o n) -> o n", o=1).broadcast_to([P, D])).then_inc(norm_rows, 16)
            split_until(FIRST_SPLIT[("q_att", 1, 0)] + AHEAD)
            for t in range(11):
                if t < 4:
                    split_until(FIRST_SPLIT[("q_att", 1, 0)] + t + 1 + AHEAD)
                if t < 8:
                    act.wait_ge(att_neg, t + 1)
                    if t - 1 > 0:
                        act.wait_ge(att_scale, t - 1)
                    for r in range(4):
                        head, tile = r % 2, r // 2
                        part = lg[:, t % 3, 3 * head * P + tile * T:3 * head * P + T + tile * P]
                        act.activation(part, part, ACT.Exp, bias=st_att[:, t % 2, 1, r:r + 1], accum_out=st_att[:, t % 2, 3, r:r + 1]).then_inc(act_chain, 1)
                        settle(act_chain)
                    act.activation(st_att[:, t % 2, 2, :], st_att[:, t % 2, 2, :], ACT.Exp).then_inc(att_exp, 1)
                    settle(att_exp)
                if 2 <= t < 10:
                    act.wait_ge(att_t, t - 1)
                    if t - 3 > 0:
                        act.wait_ge(att_o, t - 3)
                    link(act.activation(pt[:, t % 2, 0:4 * P], SB[2][:, :], ACT.Copy))
                    act.activation(pt[:, t % 2, 4 * P:6 * P], SB[3][:, 0:2 * P], ACT.Copy).then_inc(att_pt, 1)
                    settle(att_pt)
                if t >= 3:
                    act.wait_ge(att_o, t - 2)
                    act.activation(ya_hi[:, t - 3, :], SB[(t - 3) % 2][:, 0:T], ACT.Copy).then_inc(att_hi, 1)
                    settle(att_hi)
            split_until(FIRST_SPLIT[("up", 0, 0)] + AHEAD)

            take_hi(xf, x_hi, 20)
            rstd(3, RMS_EPS)
            for c in range(9):
                if c < 8:
                    split_until(FIRST_SPLIT[("up", c, 0)] + 4 + AHEAD)
                    group_ready("up", c)
                    bank = pair_of("up", c)
                    if c - 1 > 0:
                        act.wait_ge(a_ready, c - 1)
                    for b in range(2):
                        act.activation(rl[:, c % 2, 2 * b * T:2 * (b + 1) * T], bank[b][:, :], ACT.Relu).then_inc(relu_done, 1)
                        settle(relu_done)
                    act.sem_inc(pair_free[PAIR[("up", c)]], 1)
                if c >= 1:
                    if c > 0:
                        act.wait_ge(squared, c)
                    act.activation(act_tiles(c - 1)[0], rl[:, (c - 1) % 2, :].rearrange("p (k t) -> p k t", k=4), ACT.Copy).then_inc(a_hi_done, 1)
                    settle(a_hi_done)
            split_until(SPLITS)
            for i in range(NT):
                act.wait_ge(mean_done, 5 + i)
                link(act.activation(mv[:, i, 2:3], mv[:, i, 1:2], ACT.Ln, bias=RMS_EPS))
                act.activation(mv[:, i, 2:3], mv[:, i, 2:3], ACT.Exp, scale=-0.5).then_inc(rstd_done, 1)
                settle(rstd_done)
            act.wait_ge(final_done, 2)
            act.dma_start(out[0, 0:P, COLS:D], zt[:, 0, COLS:D]).then_inc(stored, 16)
            act.wait_ge(final_done, 4)
            act.dma_start(out[0, P:T, COLS:D], zt[:, 1, COLS:D]).then_inc(stored, 16)
            act.wait_ge(stored, 64)

        @block.vector
        def _(vec):
            raised = {}

            def link(ins, sem_=vec_chain):
                ins.then_inc(sem_, 1)
                settle(sem_)

            def settle(sem_):
                raised[id(sem_)] = raised.get(id(sem_), 0) + 1
                vec.wait_ge(sem_, raised[id(sem_)])

            def group_ready(name, i):
                if (name, i) in UNITS_DONE:
                    vec.wait_ge(split_used, UNITS_DONE[(name, i)])
                else:
                    vec.wait_ge(turned, TURNED[(name, i)])

            def free(name, i):
                vec.sem_inc(pair_free[PAIR[(name, i)]], 1)

            def take(name, first, src, hi, lo, base, gain=None, offset=None, parts=range(4)):
                def low(b):
                    vec.wait_ge(xhi_done, base + b + 1)
                    vec.tensor_tensor(lo[:, 2 * b:2 * b + 2, :], src[:, b % 2, :].rearrange("p (k t) -> p k t", k=2),
                        hi[:, 2 * b:2 * b + 2, :].bitcast(F32), ALU.subtract).then_inc(x_ready, 1)
                    settle(x_ready)

                for b in parts:
                    c, half = b // 2, b % 2
                    if half == 0:
                        group_ready(name, first + c)
                    bank = pair_of(name, first + c)[half]
                    if gain is None:
                        vec.tensor_copy(src[:, b % 2, :], bank[:, :]).then_inc(xf_done, 1)
                        settle(xf_done)
                    else:
                        for j in range(2):
                            k = 2 * b + j
                            o, i_ = src[:, b % 2, j * T:(j + 1) * T], bank[:, j * T:(j + 1) * T]
                            sig = xf_done if j else vec_chain
                            if offset is None:
                                link(vec.tensor_scalar(o, i_, colB[:, gain + k:gain + k + 1], None, ALU.mult), sig)
                            else:
                                link(vec.tensor_scalar(o, i_, colB[:, gain + k:gain + k + 1], colB[:, offset + k:offset + k + 1],
                                    ALU.mult, ALU.add), sig)
                    if half == 1:
                        free(name, first + c)
                    if b > parts[0]:
                        low(b - 1)
                low(parts[-1])

            for z_, w_ in ((pad[:, :, 0:3], 3), (upad[:, 0:2], 2)):
                link(vec.memset(z_, 0.0))
            take("x_t", 0, xf0, x_hi, x_lo, 0, parts=range(2))
            take("x_t", 0, xf0, x_hi, x_lo, 0, parts=range(2, 4))
            vec.wait_ge(tail_split, 1)
            vec.tensor_tensor(tail_lo[:, :, :], tail_w[:, :, :], tail_hi[:, :, :].bitcast(F32), ALU.subtract).then_inc(tail_low, 1)
            settle(tail_low)

            vec.wait_ge(stack_t, 1)
            vec.tensor_copy(colA[:, :], SB[0][:, 0:STACK_A]).then_inc(cols_taken, 1)
            settle(cols_taken)

            def gates():
                vec.wait_ge(tail_copied, 1)
                vec.wait_ge(rows_loaded, 32)
                link(vec.tensor_tensor(gt[:, 1, :, :], gt[:, 1, :, :], gate_rows[:, 1, :].unsqueeze(1).broadcast_to([P, NT, GH]), ALU.add))
                link(vec.tensor_scalar(gt[:, 4, :, :], gt[:, 1, :, :], -1.0, None, ALU.mult))
                vec.tensor_tensor(gt[:, 4, :, :], gt[:, 4, :, :], gt[:, 1, :, :], ALU.min).then_inc(gates_abs, 1)
                settle(gates_abs)
                vec.wait_ge(gates_tanh, 1)
                link(vec.tensor_scalar(gt[:, 2, :, :], gt[:, 2, :, :], 1.0, 0.5, ALU.add, ALU.mult))
                link(vec.tensor_scalar(gt[:, 3, :, :], gt[:, 2, :, :], 0.5, None, ALU.mult))
                vec.wait_ge(gates_log, 1)
                link(vec.scalar_tensor_tensor(gt[:, 5, :, :], gt[:, 1, :, :], 0.0, gt[:, 4, :, :], ALU.max, ALU.add))
                vec.scalar_tensor_tensor(gt[:, 5, :, :], gt[:, 5, :, :], -1.0,
                    gate_rows[:, 0, :].unsqueeze(1).broadcast_to([P, NT, GH]), ALU.mult, ALU.mult).then_inc(gates_ready, 1)
                settle(gates_ready)

            def heads(g, row, half):
                return gt[:, row, g, 4 * half:4 * half + 4].unsqueeze(2).broadcast_to([P, 4, P])

            def four(ap):
                return ap.rearrange("p (u c) -> p u c", u=4)

            def all4(m):
                return m.unsqueeze(1).broadcast_to([P, 4, P])

            def gate_products(half):
                for g in range(2):
                    link(vec.tensor_tensor(four(GAF[:, g, :]), all4(after), heads(g, 5, half), ALU.mult), gdn_gates if g else vec_chain)

            def normalise(h):
                vec.wait_ge(norm_rs, h + 1)
                rs = (XN, XT)[h % 4 // 2][:, h % 2, :]
                link(vec.scalar_tensor_tensor(qT[:, h, :], qT[:, h, :], P ** -0.5, rs[:, 0:T], ALU.mult, ALU.mult))
                vec.tensor_tensor(kT[:, h, :], kT[:, h, :], rs[:, T:2 * T], ALU.mult).then_inc(norm_done, 1)
                settle(norm_done)

            for h in range(GH):
                if h == 1:
                    gates()
                if h == 3:
                    vec.wait_ge(stack_t, 2)
                    vec.tensor_copy(colB[:, :], SB[2][:, 0:STACK_B]).then_inc(cols_taken, 1)
                    settle(cols_taken)
                    link(vec.tensor_scalar(colB[:, CONV_A:CONV_A + 24], colB[:, CONV_A:CONV_A + 24], 0.5, None, ALU.mult))
                    link(vec.tensor_scalar(colB[:, GDNG:HGRNG + 1], colB[:, GDNG:HGRNG + 1], 0.5, None, ALU.mult))
                vec.wait_ge(conv_copied, 2 * h + 2)
                for s in range(3):
                    o = cv[:, s * T:(s + 1) * T]
                    for tap in range(4):
                        w = colA[:, tap * 24 + s * 8 + h:tap * 24 + s * 8 + h + 1]
                        x_ = pad[:, s, tap:tap + T]
                        if tap == 0:
                            link(vec.tensor_scalar(o, x_, w, None, ALU.mult))
                        else:
                            link(vec.scalar_tensor_tensor(o, x_, w, o, ALU.mult, ALU.add), conv_done if (s, tap) == (2, 3) else vec_chain)
                vec.wait_ge(z_tanh, h + 1)
                link(vec.scalar_tensor_tensor(szb[:, h, :], thz[:, :], 1.0, pair_of("qkvz", h)[1][:, T:2 * T], ALU.add, ALU.mult))
                free("qkvz", h)
                vec.wait_ge(conv_tanh, h + 1)
                for s, dst in enumerate((qT, kT, vT)):
                    link(vec.scalar_tensor_tensor(dst[:, h, :], th[:, s * T:(s + 1) * T], 1.0, cv[:, s * T:(s + 1) * T], ALU.add,
                        ALU.mult), qkv_done if s == 2 else vec_chain)
                if h == 5:
                    gate_products(0)
                if h == 6:
                    normalise(0)
                    normalise(1)
            vec.wait_ge(gate_exp, 1)
            link(vec.tensor_copy(gt[:, 7, 0, :], gt[:, 6, 0, :]))
            link(vec.tensor_tensor(gt[:, 7, 1, :], gt[:, 6, 1, :], gt[:, 2, 1, :], ALU.mult))

            for m in range(2, GH):
                normalise(m)

            def columns(ap, s, which):
                return ap.rearrange("p (n t r) -> p n t r", t=2, r=s)[:, :, which, :]

            def gdn(half, s):
                for g in range(2):
                    if (s, g) not in DVE_STEPS:
                        continue
                    vec.wait_ge(gdn_products, pe_step(half, s, g))
                    A, B, V = SB[2 * g], SB[2 * g + 1], "gdn_vector"
                    if s == 0:
                        vec.wait_ge(gdn_exp, 3 * half + g + 1)
                        link(vec.tensor_tensor(four(EL[:, g, :]), four(EL[:, g, :]), heads(g, 2, half), ALU.mult))
                        vec.tensor_tensor(four(AT[:, g, :]), four(AT[:, g, :]), all4(upto), ALU.mult).then_inc(gdn_vector, 1)
                        settle(gdn_vector)
                    elif s == 1:
                        link(vec.tensor_tensor(EL[:, g, :], A[:, :], EL[:, g, :], ALU.mult))
                        vec.tensor_tensor(AT[:, g, :], B[:, :], AT[:, g, :], ALU.mult).then_inc(gdn_vector, 1)
                        settle(gdn_vector)
                    elif s == 2:
                        if g == 1:
                            vec.wait_ge(gdn_exp, 3 * half + 3)
                            link(vec.tensor_tensor(four(QD[:, 1, :]), qT[:, 4 * half:4 * half + 4, P:T], four(QD[:, 0, :]), ALU.mult))
                        vec.tensor_copy(LT[:, g, :], A[:, :]).then_inc(gdn_vector, 1)
                        settle(gdn_vector)
                        link(vec.tensor_tensor(four(XN[:, g, :]), four(EL[:, g, :]), all4(neg[1]), ALU.mult))
                        link(vec.tensor_tensor(four(XN[:, g, :]), four(XN[:, g, :]), all4(ident), ALU.add))
                        link(vec.tensor_tensor(four(XT[:, g, :]), four(LT[:, g, :]), all4(neg1t), ALU.mult))
                        link(vec.tensor_tensor(four(XT[:, g, :]), four(XT[:, g, :]), all4(ident), ALU.add))
                    elif s == 3:
                        link(vec.tensor_tensor(four(KX[:, g, :]), four(A[:, :]), heads(g, 7, half), ALU.mult))
                        vec.tensor_tensor(four(VB[:, g, :]), four(B[:, :]), heads(g, 3, half), ALU.mult).then_inc(gdn_vector, 1)
                        settle(gdn_vector)
                    elif s < 16:
                        lv = LEVELS[(s - 4) // 2 + 1]
                        if s % 2 == 0:
                            vec.tensor_tensor(four(EL[:, g, :]), four(A[:, :]), all4(neg[lv]), ALU.mult).then_inc(gdn_vector, 1)
                            settle(gdn_vector)
                        else:
                            if s != 15:
                                o = columns(XN[:, g, :], lv, 0)
                                link(vec.tensor_tensor(o, B[:, 0:256].rearrange("p (n r) -> p n r", r=lv), o, ALU.add))
                            o = columns(XT[:, g, :], lv, 1)
                            vec.tensor_tensor(o, B[:, 256:512].rearrange("p (n r) -> p n r", r=lv), o, ALU.add).then_inc(gdn_vector, 1)
                            settle(gdn_vector)
                    elif s == 16 and g == 0:
                        vec.tensor_copy(XN[:, 0, :], A[:, :]).then_inc(gdn_vector, 1)
                        settle(gdn_vector)
                    elif s == 16:
                        vec.tensor_scalar(LT[:, 1, :], A[:, :], -1.0, None, ALU.mult).then_inc(gdn_vector, 1)
                        settle(gdn_vector)
                    elif s == 17:
                        vec.tensor_copy(LT[:, 0, :], B[:, :]).then_inc(gdn_vector, 1)
                        settle(gdn_vector)
                    elif s == 18:
                        vec.tensor_copy(XN[:, 1, :], A[:, :]).then_inc(gdn_vector, 1)
                        settle(gdn_vector)
                    elif s == 20:
                        vec.wait_ge(gdn_rstd, 2 * half + g + 1)
                        hh = 4 * half + 2 * g
                        vec.tensor_tensor(VB[:, g, :], A[:, :], KX[:, g, :], ALU.mult).then_inc(gdn_vector, 1)
                        settle(gdn_vector)
                        y = VB[:, g, :].rearrange("p (h t) -> p h t", h=2)
                        vec.scalar_tensor_tensor(y, y, colB[:, GDNG:GDNG + 1], szb[:, hh:hh + 2, :], ALU.mult, ALU.mult).then_inc(gdn_gated, 1)
                        settle(gdn_gated)
                if s == 20:
                    for g in range(2):
                        vec.wait_ge(gdn_hi, 2 * half + g + 1)
                        hh = 4 * half + 2 * g
                        vec.tensor_tensor(yb_lo[:, hh:hh + 2, :], VB[:, g, :].rearrange("p (h t) -> p h t", h=2),
                            yb_hi[:, hh:hh + 2, :].bitcast(F32), ALU.subtract).then_inc(gdn_ready, 1)
                        settle(gdn_ready)

            def ya(j):
                vec.wait_ge(h_copied, 2 * j + 2)
                bank = pair_of("hcbz", j)
                link(vec.tensor_tensor(upad[:, 2:T + 2], bank[0][:, T:2 * T], hs[:, :], ALU.mult))
                for tap in range(3):
                    w = colB[:, CONV_A + tap * 8 + j:CONV_A + tap * 8 + j + 1]
                    if tap == 0:
                        link(vec.tensor_scalar(yf[:, :], upad[:, 0:T], w, None, ALU.mult))
                    else:
                        link(vec.scalar_tensor_tensor(yf[:, :], upad[:, tap:tap + T], w, yf[:, :], ALU.mult, ALU.add))
                link(vec.tensor_tensor(yf[:, :], bank[1][:, 0:T], yf[:, :], ALU.mult))
                link(vec.scalar_tensor_tensor(hs[:, :], thz[:, :], 1.0, bank[1][:, T:2 * T], ALU.add, ALU.mult))
                free("hcbz", j)
                vec.tensor_tensor(yf[:, :], yf[:, :], hs[:, :], ALU.mult).then_inc(ya_done, 1)
                settle(ya_done)

            def ya_low(j):
                vec.wait_ge(ya_hi_done, j + 1)
                vec.tensor_tensor(ya_lo[:, j, :], yf[:, :], ya_hi[:, j, :].bitcast(F32), ALU.subtract).then_inc(ya_ready, 1)
                settle(ya_ready)

            vec.wait_ge(consts_loaded, 32)
            for half in range(2):
                for s in range(GSTEPS):
                    slot = half * GSTEPS + s
                    if slot < 32 and slot % 4 == 2:
                        ya_low(slot // 4)
                    gdn(half, s)
                    if slot == 10:
                        gate_products(1)
                    if slot < 32 and slot % 4 == 0:
                        ya(slot // 4)

            def take_p(layer):
                vec.wait_ge(p_t, layer + 1)
                vec.tensor_copy(pf[:, :, :], SB[0][:, :].rearrange("p (k t) -> p k t", k=2)).then_inc(pf_done, 1)
                settle(pf_done)
                vec.wait_ge(p_hi_done, layer + 1)
                vec.tensor_tensor(p_lo[:, :, :], pf[:, :, :], p_hi[:, :, :].bitcast(F32), ALU.subtract).then_inc(p_ready, 1)
                settle(p_ready)

            def part_stats(c, i):
                link(vec.bn_stats(stats[:, i, c, :], xtok[:, i, c * COLS:(c + 1) * COLS]))

            def residual(name, alpha, layer=None, turn=None):
                for c in range(2):
                    group_ready(name, c)
                    bank = pair_of(name, c)
                    for i in range(NT):
                        o = xtok[:, i, c * COLS:(c + 1) * COLS]
                        vec.scalar_tensor_tensor(o, o, alpha, bank[i][:, :], ALU.mult, ALU.add).then_inc(r_done, 1)
                        settle(r_done)
                    free(name, c)
                    if turn is not None:
                        turn(c)
                    for i in range(NT):
                        part_stats(c, i)
                    if c == 0 and layer is not None:
                        take_p(layer)

            def row_stats(squares):
                for i in range(NT):
                    link(vec.bn_aggr(mv[:, i, 0:2], stats[:, i, :, :].rearrange("p c s -> p (c s)")), mean_done if i and not squares else vec_chain)
                if squares:
                    link(vec.tensor_tensor(mv[:, :, 3:4], mv[:, :, 0:1], mv[:, :, 0:1], ALU.mult))
                    vec.tensor_tensor(mv[:, :, 1:2], mv[:, :, 1:2], mv[:, :, 3:4], ALU.add).then_inc(mean_done, 1)
                    settle(mean_done)

            def layer_end(layer):
                residual(("out_even", "out_odd")[layer], ALPHA, layer)
                row_stats(False)
                vec.wait_ge(rstd_done, layer + 1)
                for c in range(2):
                    for i in range(NT):
                        cols = slice(c * COLS, (c + 1) * COLS)
                        vec.tensor_scalar(zt[:, i, cols], xtok[:, i, cols], mv[:, i, 0:1], mv[:, i, 2:3], ALU.subtract, ALU.mult).then_inc(z_ready, 1)
                        settle(z_ready)
                take("ln_t", 2 * layer, xf, ya_hi, ya_lo, 4 + 8 * layer, LNG + 8 * layer, LNB + 8 * layer)
                vec.wait_ge(norm_rows, 32 * (layer + 1))
                for i in range(NT):
                    link(vec.tensor_tensor(xtok[:, i, :], zt[:, i, :], gb[:, 0, :], ALU.mult))
                    link(vec.tensor_tensor(xtok[:, i, :], xtok[:, i, :], gb[:, 1, :], ALU.add))
                vec.wait_ge(split_used, FIRST_SPLIT[("pl", layer, 0)] + 2)
                for c in range(2):
                    for i in range(NT):
                        vec.wait_ge(gate_tanh, 4 * layer + 2 * c + i + 1)
                        link(vec.scalar_tensor_tensor(eg[:, i, :], eg[:, i, :], 1.0, SB[2 * i + c][:, :], ALU.add, ALU.mult))
                        o = xtok[:, i, c * COLS:(c + 1) * COLS]
                        link(vec.scalar_tensor_tensor(o, eg[:, i, :], 0.5, o, ALU.mult, ALU.add), x2_done if i else vec_chain)
                    free("gate", 2 * layer + c)
                    if layer == 0:
                        take("x2_t", 0, xf, x_hi, x_lo, 8, parts=range(2 * c, 2 * c + 2))
                    else:
                        take("att_t", 0, xf, x_hi, x_lo, 16, ATTN, parts=range(2 * c, 2 * c + 2))
                        for i in range(NT):
                            part_stats(c, i)

            layer_end(0)

            for i in range(2):
                link(vec.memset(AA[:, i, :], 0.0))
            l0, l1 = colB[:, LB:LB + HH], colB[:, LB + HH:LB + 2 * HH]
            link(vec.tensor_tensor(lbc[:, 2, :], l0, l1, ALU.max))
            link(vec.tensor_tensor(lbc[:, 0, :], l0, lbc[:, 2, :], ALU.subtract))
            vec.tensor_tensor(lbc[:, 1, :], l1, lbc[:, 2, :], ALU.subtract).then_inc(lb_diff, 1)
            settle(lb_diff)
            vec.wait_ge(lb_exp, 1)
            link(vec.tensor_tensor(lbc[:, 2, :], lbc[:, 0, :], lbc[:, 1, :], ALU.add))
            link(vec.reciprocal(lbc[:, 3, :], lbc[:, 2, :]))
            link(vec.tensor_tensor(lbc[:, 3, :], lbc[:, 3, :], lbc[:, 1, :], ALU.mult))
            link(vec.tensor_scalar(lbc[:, 4, :], lbc[:, 3, :], 0.5, 0.5, ALU.mult, ALU.add))
            vec.tensor_scalar(lbc[:, 5, :], lbc[:, 3, :], -0.5, 0.5, ALU.mult, ALU.add).then_inc(lb_done, 1)
            settle(lb_done)

            def hg_gate(h):
                p, i = h // 2, h % 2
                par, cols = p % 2, slice(i * T, (i + 1) * T)
                vec.wait_ge(hg_act, h + 1)
                if p - 1 > 0:
                    vec.wait_ge(hg_cross_mm, p - 1)
                bank = pair_of("qfiz", h)
                link(vec.scalar_tensor_tensor(q0[:, par, cols], qfth[:, i, 0:T], 1.0, bank[0][:, 0:T], ALU.add, ALU.mult))
                link(vec.scalar_tensor_tensor(szo[:, p % 3, cols], zth[:, i, :], 1.0, bank[1][:, T:2 * T], ALU.add, ALU.mult))
                free("qfiz", h)
                link(vec.tensor_scalar(F0[:, par, cols], qfth[:, i, T:2 * T], lbc[:, 5, h:h + 1], lbc[:, 4, h:h + 1], ALU.mult, ALU.add))
                link(vec.tensor_scalar(KS[:, par, cols], F0[:, par, cols], -1.0, 1.0, ALU.mult, ALU.add))
                vec.tensor_tensor(QS[:, par, cols], q0[:, par, cols], F0[:, par, cols], ALU.mult).then_inc(hg_gated, 1)
                settle(hg_gated)

            f_at = {1: 0}
            for n, s in enumerate(LEVELS[1:]):
                f_at[s] = sum(2 * T // x for x in LEVELS[1:1 + n])

            def decay(par, s, which):
                blocks = F0[:, par, :] if s == 1 else F1[:, f_at[s]:f_at[s] + 2 * T // s]
                return blocks.rearrange("p (n t) -> p n t", t=2)[:, :, which:which + 1]

            def level(par, L, k):
                s = LEVELS[k - 1]
                vec.wait_ge(hg_level_mm, 7 * L + k)
                n_ = 64 // s
                n2 = 2 * T // (2 * s)
                o = columns(QS[:, par, :], s, 1)
                link(vec.tensor_tensor(o, o, decay(par, s, 0).broadcast_to([P, n2, s]), ALU.mult))
                o = columns(KS[:, par, :], s, 0)
                vec.tensor_tensor(o, o, decay(par, s, 1).broadcast_to([P, n2, s]), ALU.mult).then_inc(hg_level, 1)
                settle(hg_level)
                if k == 1:
                    link(vec.copy_predicated(four(AA[:, par, :]), all4(ident).bitcast(I32), four(SB[0][:, :])))
                o = AA[:, par, :].rearrange("p (u m t r) -> p u m t r", u=4, t=2, r=s)[:, :, :, 1, :]
                m = pick[s].rearrange("p (m r) -> p m r", r=s).unsqueeze(1).broadcast_to([P, 4, n_, s])
                vec.copy_predicated(o, m, SB[k % 2][:, 0:256].rearrange("p (u m r) -> p u m r", u=4, r=s)).then_inc(hg_picked, 1)
                settle(hg_picked)
                if s < 64:
                    link(vec.tensor_tensor(F1[:, f_at[2 * s]:f_at[2 * s] + n2].unsqueeze(2), decay(par, s, 0), decay(par, s, 1), ALU.mult))

            for it in range(HH // 2 + 2):
                L, C = it - 1, it - 2
                for k in range(8):
                    if k == 0 and 0 <= L < HH // 2:
                        hg_gate(2 * L + 1)
                        vec.wait_ge(hg_vt, L + 1)
                        if L - 1 > 0:
                            vec.wait_ge(hg_o, L - 1)
                        vec.tensor_copy(vtok[:, L % 2, :], SB[2][:, :]).then_inc(hg_vt_taken, 1)
                        settle(hg_vt_taken)
                    if k == 0 and 0 <= C < HH // 2:
                        vec.wait_ge(hg_cross_mm, C + 1)
                        vec.tensor_copy(CR[:, C % 2, :], SB[0][:, 0:2 * P]).then_inc(hg_cross, 1)
                        settle(hg_cross)
                    if k >= 1 and 0 <= L < HH // 2:
                        level(L % 2, L, k)
                    if k == 4 and it < HH // 2:
                        hg_gate(2 * it)
                    if k == 3 and 0 <= C < HH // 2:
                        vec.wait_ge(hg_rs, C + 1)
                        link(vec.tensor_tensor(yo[:, :], SB[3][:, :], rso[:, :], ALU.mult))
                        vec.scalar_tensor_tensor(yo[:, :], yo[:, :], colB[:, HGRNG:HGRNG + 1], szo[:, C % 3, :], ALU.mult, ALU.mult).then_inc(hg_y, 1)
                        settle(hg_y)
                    if k == 5 and 0 <= C < HH // 2:
                        vec.wait_ge(hg_hi, C + 1)
                        hi, lo = ((ya_hi, ya_lo), (yb_hi, yb_lo))[C // 4]
                        tiles = slice(2 * (C % 4), 2 * (C % 4) + 2)
                        vec.tensor_tensor(lo[:, tiles, :], yo[:, :].rearrange("p (h t) -> p h t", h=2), hi[:, tiles, :].bitcast(F32),
                            ALU.subtract).then_inc(hg_ready, 1)
                        settle(hg_ready)
            layer_end(1)

            def take_root_row(n):
                vec.wait_ge(row_spread, n)
                link(vec.tensor_copy(root[:, :], SB[0][:, 0:T]))

            def queries(c):
                group_ready("q_att", c)
                bank = pair_of("q_att", c)
                for b in range(2):
                    vec.scalar_tensor_tensor(qa[:, 4 * c + 2 * b:4 * c + 2 * b + 2, :], bank[b][:, :].rearrange("p (k t) -> p k t", k=2),
                        AD ** -0.5, root[:, :].unsqueeze(1).broadcast_to([P, 2, T]), ALU.mult, ALU.mult).then_inc(att_in, 1)
                    settle(att_in)
                free("q_att", c)

            row_stats(True)
            take_root_row(1)
            queries(0)
            group_ready("kv_att", 0)
            bank = pair_of("kv_att", 0)
            vec.tensor_tensor(ka[:, :, :], bank[0][:, :].rearrange("p (k t) -> p k t", k=2),
                root[:, :].unsqueeze(1).broadcast_to([P, 2, T]), ALU.mult).then_inc(att_in, 1)
            settle(att_in)
            link(vec.tensor_scalar(va[:, 0, :], bank[1][:, 0:P], mv[:, 0, 2:3], None, ALU.mult))
            vec.tensor_scalar(va[:, 1, :], bank[1][:, P:2 * P], mv[:, 1, 2:3], None, ALU.mult).then_inc(att_in, 1)
            settle(att_in)
            free("kv_att", 0)
            vec.wait_ge(sinks_loaded, 16)
            link(vec.tensor_scalar(nsink[:, :], sink_row[:, :], -1.0, None, ALU.mult))

            def scores(t):
                group_ready("score", t)
                bank = pair_of("score", t)
                par = t % 2
                if t - 2 > 0:
                    vec.wait_ge(att_t, t - 2)
                for j in range(2):
                    link(vec.scalar_tensor_tensor(lg[:, t % 3, 3 * j * P:3 * (j + 1) * P], ndist, 2.0 ** (-8.0 * (2 * t + j + 1) / AH),
                        bank[j][:, 0:3 * P], ALU.mult, ALU.add))
                free("score", t)
                rows = lg[:, t % 3, :].rearrange("p (h c) -> p h c", h=2)
                link(vec.tensor_reduce(st_att[:, par, 0, 0:2], rows[:, :, 0:2 * P], AX_X, ALU.max))
                link(vec.tensor_reduce(st_att[:, par, 0, 2:4], rows[:, :, 2 * P:3 * P], AX_X, ALU.max))
                two = [x[:, 2 * t:2 * t + 2].unsqueeze(1).broadcast_to([P, 2, 2]) for x in (sink_row, nsink)]
                mx, ng, ex = [st_att[:, par, i, :].rearrange("p (b h) -> p b h", b=2) for i in range(3)]
                link(vec.scalar_tensor_tensor(ng, mx, -1.0, two[1], ALU.mult, ALU.min))
                vec.tensor_tensor(ex, two[0], ng, ALU.add).then_inc(att_neg, 1)
                settle(att_neg)

            def scales(t):
                par = t % 2
                vec.wait_ge(att_exp, t + 1)
                link(vec.tensor_tensor(st_att[:, par, 3, :], st_att[:, par, 3, :], st_att[:, par, 2, :], ALU.add))
                if t - 1 > 0:
                    vec.wait_ge(att_scale, t - 1)
                vec.reciprocal(rsum[:, par, :], st_att[:, par, 3, :]).then_inc(att_root, 1)
                settle(att_root)

            for t in range(13):
                if t >= 5:
                    r = t - 5
                    vec.wait_ge(att_hi, r + 1)
                    vec.tensor_tensor(ya_lo[:, r, :], SB[r % 2][:, 0:T], ya_hi[:, r, :].bitcast(F32), ALU.subtract).then_inc(att_ready, 1)
                    settle(att_ready)
                if t < 8:
                    scores(t)
                if 1 <= t < 9:
                    scales(t - 1)
                if t == 3:
                    queries(1)
            residual("o_att", 1.0, turn=lambda c: take("mlp_t", 0, xf, x_hi, x_lo, 20, MLPN, parts=range(2 * c, 2 * c + 2)))
            row_stats(True)
            take_root_row(2)
            link(vec.tensor_tensor(root[:, :], root[:, :], root[:, :], ALU.mult))
            for c in range(9):
                if c < 8:
                    vec.wait_ge(relu_done, 2 * c + 2)
                    link(vec.tensor_tensor(rl[:, c % 2, :], rl[:, c % 2, :], rl[:, c % 2, :], ALU.mult))
                    four_tiles = rl[:, c % 2, :].rearrange("p (k t) -> p k t", k=4)
                    vec.tensor_tensor(four_tiles, four_tiles, root[:, :].unsqueeze(1).broadcast_to([P, 4, T]), ALU.mult).then_inc(squared, 1)
                    settle(squared)
                if c >= 1:
                    if c > 0:
                        vec.wait_ge(a_hi_done, c)
                    hi, lo = act_tiles(c - 1)
                    vec.tensor_tensor(lo, rl[:, (c - 1) % 2, :].rearrange("p (k t) -> p k t", k=4), hi.bitcast(F32),
                        ALU.subtract).then_inc(a_ready, 1)
                    settle(a_ready)
            for c in range(2):
                group_ready("down", c)
                for i in range(NT):
                    o = xtok[:, i, c * COLS:(c + 1) * COLS]
                    link(vec.tensor_tensor(o, o, pair_of("down", c)[i][:, :], ALU.add))
                    part_stats(c, i)
                    if c == 1:
                        link(vec.bn_aggr(mv[:, i, 0:2], stats[:, i, :, :].rearrange("p c s -> p (c s)")))
                        vec.scalar_tensor_tensor(mv[:, i, 1:2], mv[:, i, 0:1], mv[:, i, 0:1], mv[:, i, 1:2], ALU.mult, ALU.add).then_inc(mean_done, 1)
                        settle(mean_done)
            vec.wait_ge(norm_rows, 80)
            for i in range(NT):
                vec.wait_ge(rstd_done, 5 + i)
                for c in range(2):
                    cols = slice(c * COLS, (c + 1) * COLS)
                    vec.scalar_tensor_tensor(zt[:, i, cols], xtok[:, i, cols], mv[:, i, 2:3], gb[:, 0, cols], ALU.mult, ALU.mult).then_inc(final_done, 1)
                    settle(final_done)


def shape_constants():
    import numpy as np

    i, j = np.arange(P)[:, None], np.arange(P)[None, :]
    out = np.zeros((P, C_ALL), np.float32)
    out[:, C_ID:C_ID + P] = i == j
    out[:, C_UPTO:C_UPTO + P] = i <= j
    out[:, C_AFTER:C_AFTER + P] = i > j
    out[:, C_ONES:C_ONES + P] = 1
    for n, s in enumerate(LEVELS):
        below = (i // s % 2 == 1) & (j // s == i // s - 1)
        out[:, C_NEG + n * P:C_NEG + (n + 1) * P] = np.where(below, -1, 0)
        out[:, C_PICK + n * 64:C_PICK + (n + 1) * 64] = below.T.reshape(P, P // (2 * s), 2, s)[:, :, 1, :].reshape(P, 64)
        if s == 1:
            out[:, C_NEG1T:C_NEG1T + P] = np.where(below.T, -1, 0)
    key = np.arange(2 * P)[None, :]
    dist = P + i - key
    out[:, C_DIST:C_DIST + 2 * P] = np.where((dist >= 0) & (dist < P), -dist, -1e30)
    out[:, C_DIST + 2 * P:C_DIST + 3 * P] = out[:, C_DIST + P:C_DIST + 2 * P]
    return out


_INS = ["x", "p", "w_in_even", "conv_a_w", "conv_b_w", "a_log", "dt_bias", "gdn_norm_g", "w_out_even", "w_in_odd",
        "lower_bounds", "hgrn_norm_g", "w_out_odd", "ln_g", "ln_b", "w_pl", "w_pl_gate", "attn_norm_2", "mlp_norm_2",
        "final_norm_2", "swa_w_qkv_2", "swa_sinks_2", "swa_w_o_2", "mlp_w_up_2", "mlp_w_down_2"]


def kernel(**inputs):
    import numpy as _np
    import concourse.bacc as _bacc
    from concourse import mybir as _mybir
    from concourse.bass_utils import run_bass_kernel_spmd as _run

    nc = _bacc.Bacc("TRN2", target_bir_lowering=False, num_devices=1)
    arrays, args = {}, {}
    for name in _INS:
        x = _np.ascontiguousarray(inputs[name])
        arrays[f"in_{name}_dram"] = x
        args[name] = nc.dram_tensor(f"in_{name}_dram", x.shape, _mybir.dt.from_np(x.dtype), kind="ExternalInput").ap()
    table = shape_constants()
    arrays["shape_constants_dram"] = table
    consts = nc.dram_tensor("shape_constants_dram", table.shape, F32, kind="ExternalInput").ap()
    out = nc.dram_tensor("out_0_dram", (1, T, D), F32, kind="ExternalOutput").ap()
    build(nc, args, consts, out)
    r = _run(nc, [arrays], core_ids=[0])
    return r.results[0]["out_0_dram"]
```
